# Optimizing a Trainium2 kernel written in Bass

```python
import jax, jax.numpy as jnp
from jax import lax
import numpy as np

D_MODEL = 1024
BATCH = 1
SEQ = 512
DEPTH = 1

CHUNK = 64
CONV_WIDTH = 3
CONV_DIM = D_MODEL // 2
CONV_GROUPS = 8
RET_HEADS = 4
RET_DIM = D_MODEL - CONV_DIM
RET_HEAD_DIM = RET_DIM // RET_HEADS
MIX_DIM = CONV_DIM + RET_DIM
IN_DIM = 3 * CONV_DIM + 4 * RET_DIM
D_FF = 4 * D_MODEL
ROPE_BASE = 10000.0
DECAY_OFFSET = 5.0
EPS = 1e-6
N_MOD = 6


def rms_norm(x, g):
    xf = x.astype(jnp.float32)
    y = xf * lax.rsqrt(jnp.mean(xf * xf, axis=-1, keepdims=True) + EPS)
    return (y * g.astype(jnp.float32)).astype(x.dtype)

def rotary(t, positions):
    half = t.shape[-1] // 2
    inv_freq = ROPE_BASE ** (-jnp.arange(half, dtype=jnp.float32) / half)
    ang = positions.astype(jnp.float32)[..., None] * inv_freq
    cos = jnp.cos(ang)[:, :, None, :]
    sin = jnp.sin(ang)[:, :, None, :]
    tf = t.astype(jnp.float32)
    t1, t2 = tf[..., :half], tf[..., half:]
    out = jnp.concatenate([t1 * cos - t2 * sin, t2 * cos + t1 * sin], axis=-1)
    return out.astype(t.dtype)

def short_conv_mixer(xin, b_gate, c_gate, conv_w):
    S = xin.shape[1]
    u = c_gate * xin
    up = jnp.pad(u, ((0, 0), (CONV_WIDTH - 1, 0), (0, 0)))
    y = up[:, 0:S] * conv_w[0]
    for j in range(1, CONV_WIDTH):
        y = y + up[:, j:j + S] * conv_w[j]
    return b_gate * y

def retention_mixer(q, k, v, g, positions):
    B, S, _ = q.shape
    H, dh, C = RET_HEADS, RET_HEAD_DIM, CHUNK
    NC = S // C
    dt = q.dtype
    q = rotary(q.reshape(B, S, H, dh), positions)
    k = rotary(k.reshape(B, S, H, dh), positions) * (dh ** -0.5)
    v = v.reshape(B, S, H, dh)

    def to_chunks(t):
        return t.reshape(B, NC, C, H, dh).transpose(0, 3, 1, 2, 4)

    q, k, v = to_chunks(q), to_chunks(k), to_chunks(v)

    log_gamma = jnp.log1p(-jnp.exp2(-DECAY_OFFSET - jnp.arange(H, dtype=jnp.float32)))
    idx = jnp.arange(C, dtype=jnp.float32)
    intra_dec = jnp.exp(log_gamma[:, None, None] * jnp.abs(idx[:, None] - idx[None, :]))
    q_dec = jnp.exp(log_gamma[:, None] * (idx + 1.0))
    k_dec = jnp.exp(log_gamma[:, None] * (C - 1.0 - idx))
    chunk_dec = jnp.exp(log_gamma * C)

    scores = jnp.einsum('bhncd,bhnmd->bhncm', q, k) * intra_dec[:, None].astype(dt)
    o_intra = jnp.einsum('bhncm,bhnmd->bhncd', scores, v)

    kv = jnp.einsum('bhnmd,bhnme->nbhde', k * k_dec[:, None, :, None].astype(dt), v)
    kv = kv.astype(jnp.float32)

    def step(state, kv_n):
        return state * chunk_dec[:, None, None] + kv_n, state

    _, s_prev = lax.scan(step, jnp.zeros((B, H, dh, dh), jnp.float32), kv)
    o_cross = jnp.einsum('bhncd,nbhde->bhnce',
                         q * q_dec[:, None, :, None].astype(dt), s_prev.astype(dt))

    o = (o_intra + o_cross).transpose(0, 2, 3, 1, 4).reshape(B, S, H, dh)
    of = o.astype(jnp.float32)
    of = of * lax.rsqrt(jnp.mean(of * of, axis=-1, keepdims=True) + EPS)
    o = of.astype(dt).reshape(B, S, RET_DIM)
    return jax.nn.silu(g) * o

def first_inputs(seed: int = 0) -> dict:
    key = jax.random.key(seed)
    ks = jax.random.split(key, 16)
    f32 = jnp.float32
    x = jax.random.normal(ks[0], (BATCH, SEQ, D_MODEL), f32)
    c = jax.random.normal(ks[1], (BATCH, D_MODEL), f32)
    offset = jax.random.randint(ks[2], (BATCH, 1), 0, 4096, dtype=jnp.int32)
    positions = offset + jnp.arange(SEQ, dtype=jnp.int32)[None, :]
    w_ada = jax.random.normal(ks[3], (DEPTH, D_MODEL, N_MOD * D_MODEL), f32) * (0.5 * D_MODEL ** -0.5)
    b_ada = jax.random.normal(ks[4], (DEPTH, N_MOD * D_MODEL), f32) * 0.01
    g_pre_mix = 1.0 + 0.05 * jax.random.normal(ks[5], (DEPTH, D_MODEL), f32)
    g_post_mix = 1.0 + 0.05 * jax.random.normal(ks[6], (DEPTH, D_MODEL), f32)
    w_in = jax.random.normal(ks[7], (DEPTH, D_MODEL, IN_DIM), f32) * D_MODEL ** -0.5
    conv_w = jax.random.normal(ks[8], (DEPTH, CONV_WIDTH, CONV_DIM), f32) * CONV_WIDTH ** -0.5
    w_out = jax.random.normal(ks[9], (DEPTH, MIX_DIM, D_MODEL), f32) * MIX_DIM ** -0.5
    g_pre_mlp = 1.0 + 0.05 * jax.random.normal(ks[10], (DEPTH, D_MODEL), f32)
    g_post_mlp = 1.0 + 0.05 * jax.random.normal(ks[11], (DEPTH, D_MODEL), f32)
    w_fc1 = jax.random.normal(ks[12], (DEPTH, D_MODEL, D_FF), f32) * D_MODEL ** -0.5
    w_fc2 = jax.random.normal(ks[13], (DEPTH, D_FF, D_MODEL), f32) * D_FF ** -0.5
    return {'x': x, 'c': c, 'positions': positions, 'w_ada': w_ada, 'b_ada': b_ada,
            'g_pre_mix': g_pre_mix, 'g_post_mix': g_post_mix, 'w_in': w_in,
            'conv_w': conv_w, 'w_out': w_out, 'g_pre_mlp': g_pre_mlp,
            'g_post_mlp': g_post_mlp, 'w_fc1': w_fc1, 'w_fc2': w_fc2}

def first_block(x, c, positions, w_ada, b_ada, g_pre_mix, g_post_mix, w_in, conv_w,
              w_out, g_pre_mlp, g_post_mlp, w_fc1, w_fc2):
    split_at = [CONV_DIM, 2 * CONV_DIM, 3 * CONV_DIM,
                3 * CONV_DIM + RET_DIM, 3 * CONV_DIM + 2 * RET_DIM, 3 * CONV_DIM + 3 * RET_DIM]
    for layer in range(DEPTH):
        mod = jax.nn.silu(c) @ w_ada[layer] + b_ada[layer]
        shift1, scale1, gate1, shift2, scale2, gate2 = [
            m[:, None, :] for m in jnp.split(mod, N_MOD, axis=-1)]

        h = rms_norm(x, g_pre_mix[layer]) * (1.0 + scale1) + shift1
        proj = h @ w_in[layer]
        xin, b_gate, c_gate, q, k, v, g = jnp.split(proj, split_at, axis=-1)
        y_conv = short_conv_mixer(xin, b_gate, c_gate, conv_w[layer])
        y_ret = retention_mixer(q, k, v, g, positions)
        mix = jnp.concatenate([y_conv, y_ret], axis=-1) @ w_out[layer]
        x = x + gate1 * rms_norm(mix, g_post_mix[layer])

        h = rms_norm(x, g_pre_mlp[layer]) * (1.0 + scale2) + shift2
        f = jnp.square(jax.nn.relu(h @ w_fc1[layer])) @ w_fc2[layer]
        x = x + gate2 * rms_norm(f, g_post_mlp[layer])
    return x


DEPTH_2 = 2

EXPAND = 2
D_INNER = EXPAND * D_MODEL
POOL_WINDOWS = (2, 4, 8, 16)
N_POOL_GROUPS = len(POOL_WINDOWS)
POOL_GROUP = D_INNER // N_POOL_GROUPS
HGRN_HEAD_DIM = 128
HGRN_HEADS = D_INNER // HGRN_HEAD_DIM
N_MIXERS = 2
N_POOL_LAYERS = (DEPTH_2 + 1) // 2
N_HGRN_LAYERS = DEPTH_2 // 2


def rms_norm_2(x, g):
    xf = x.astype(jnp.float32)
    y = xf * lax.rsqrt(jnp.mean(xf * xf, axis=-1, keepdims=True) + EPS)
    return (y * g.astype(jnp.float32)).astype(x.dtype)

def multiscale_pool(v):
    T = v.shape[1]
    vf = v.astype(jnp.float32)
    cs = jnp.cumsum(vf, axis=1)
    pos = jnp.arange(T, dtype=jnp.float32)
    outs = []
    for g, w in enumerate(POOL_WINDOWS):
        lo, hi = g * POOL_GROUP, (g + 1) * POOL_GROUP
        c = cs[..., lo:hi]
        prev = jnp.pad(c[:, :-w], ((0, 0), (w, 0), (0, 0)))
        cnt = jnp.minimum(pos + 1.0, float(w))[None, :, None]
        outs.append((c - prev) / cnt - vf[..., lo:hi])
    return jnp.stack(outs, axis=2).astype(v.dtype)

def pool_mixer(h, w_in, w_grp, scale, w_out):
    B, T, _ = h.shape
    u = h @ w_in
    v, gate = jnp.split(u, 2, axis=-1)
    p = multiscale_pool(v)
    m = jnp.einsum('btgc,gcd->btgd', p, w_grp).reshape(B, T, D_INNER) * scale
    return (m * jax.nn.silu(gate)) @ w_out

def hgrn2_chunk_scan(q, k, v, b):
    _, Bn, H, C, dk = q.shape
    dv = v.shape[-1]
    causal = jnp.tril(jnp.ones((C, C), dtype=bool))

    def step(S, xs):
        qc, kc, vc, bc = xs
        diff = bc[:, :, :, None, :] - bc[:, :, None, :, :]
        diff = jnp.where(causal[None, None, :, :, None], diff, -jnp.inf)
        A = jnp.einsum('bhtd,bhsd,bhtsd->bhts', qc, kc, jnp.exp(diff))
        o = (jnp.einsum('bhts,bhsv->bhtv', A, vc)
             + jnp.einsum('bhtd,bhdv->bhtv', qc * jnp.exp(bc), S))
        b_last = bc[:, :, -1:, :]
        S = (jnp.exp(b_last[:, :, 0, :])[..., None] * S
             + jnp.einsum('bhsd,bhsv->bhdv', kc * jnp.exp(b_last - bc), vc))
        return S, o

    S0 = jnp.zeros((Bn, H, dk, dv), jnp.float32)
    _, o = lax.scan(step, S0, (q, k, v, b))
    return o

def hgrn2_mixer(h, w_in, lb, norm_g, w_out):
    B, T, _ = h.shape
    N = T // CHUNK
    u = h @ w_in
    q, fz, i, gate = jnp.split(u, 4, axis=-1)
    fz = fz.astype(jnp.float32)
    lbf = lb.astype(jnp.float32)
    log_f = jnp.logaddexp(jnp.log(lbf), jnp.log1p(-lbf) + jax.nn.log_sigmoid(fz))
    k = (1.0 - lbf) * jax.nn.sigmoid(-fz)

    def to_chunks(a):
        return a.astype(jnp.float32).reshape(B, N, CHUNK, HGRN_HEADS, HGRN_HEAD_DIM).transpose(1, 0, 3, 2, 4)

    qc, kc, vc, lfc = to_chunks(q), to_chunks(k), to_chunks(i), to_chunks(log_f)
    bc = jnp.cumsum(lfc, axis=3)
    o = hgrn2_chunk_scan(qc, kc, vc, bc)
    o = o.transpose(1, 0, 3, 2, 4).reshape(B, T, HGRN_HEADS, HGRN_HEAD_DIM)
    o = o * lax.rsqrt(jnp.mean(o * o, axis=-1, keepdims=True) + EPS)
    o = (o * norm_g.astype(jnp.float32).reshape(HGRN_HEADS, HGRN_HEAD_DIM)).reshape(B, T, D_INNER)
    o = o.astype(h.dtype)
    return (o * jax.nn.silu(gate)) @ w_out

def second_inputs(seed: int = 0) -> dict:
    key = jax.random.key(seed)
    ks = jax.random.split(key, 12)
    f32 = jnp.float32
    x = jax.random.normal(ks[0], (BATCH, SEQ, D_MODEL), f32)
    norm_g = 1.0 + 0.05 * jax.random.normal(ks[1], (DEPTH_2, D_MODEL), f32)
    pool_w_in = jax.random.normal(ks[2], (N_POOL_LAYERS, D_MODEL, 2 * D_INNER), f32) * D_MODEL ** -0.5
    pool_w_grp = jax.random.normal(ks[3], (N_POOL_LAYERS, N_POOL_GROUPS, POOL_GROUP, POOL_GROUP), f32) * POOL_GROUP ** -0.5
    pool_scale = 1.0 + 0.1 * jax.random.normal(ks[4], (N_POOL_LAYERS, D_INNER), f32)
    pool_w_out = jax.random.normal(ks[5], (N_POOL_LAYERS, D_INNER, D_MODEL), f32) * D_INNER ** -0.5
    hgrn_w_in = jax.random.normal(ks[6], (N_HGRN_LAYERS, D_MODEL, 4 * D_INNER), f32) * D_MODEL ** -0.5
    hgrn_lower_bounds = 0.5 * jax.random.normal(ks[7], (DEPTH_2, D_INNER), f32)
    hgrn_norm_g = 1.0 + 0.05 * jax.random.normal(ks[8], (N_HGRN_LAYERS, D_INNER), f32)
    hgrn_w_out = jax.random.normal(ks[9], (N_HGRN_LAYERS, D_INNER, D_MODEL), f32) * D_INNER ** -0.5
    final_g = 1.0 + 0.05 * jax.random.normal(ks[10], (D_MODEL,), f32)
    return {"x": x, "norm_g": norm_g, "pool_w_in": pool_w_in, "pool_w_grp": pool_w_grp,
            "pool_scale": pool_scale, "pool_w_out": pool_w_out, "hgrn_w_in": hgrn_w_in,
            "hgrn_lower_bounds": hgrn_lower_bounds, "hgrn_norm_g": hgrn_norm_g,
            "hgrn_w_out": hgrn_w_out, "final_g": final_g}

def second_block(x, norm_g, pool_w_in, pool_w_grp, pool_scale, pool_w_out, hgrn_w_in,
              hgrn_lower_bounds, hgrn_norm_g, hgrn_w_out, final_g):
    p = jax.nn.softmax(hgrn_lower_bounds.astype(jnp.float32), axis=0)
    lbs = jnp.cumsum(p, axis=0) - p[0:1]
    h = x
    for layer in range(DEPTH_2):
        hn = rms_norm_2(h, norm_g[layer])
        j = layer // N_MIXERS
        if layer % N_MIXERS == 0:
            y = pool_mixer(hn, pool_w_in[j], pool_w_grp[j], pool_scale[j], pool_w_out[j])
        else:
            y = hgrn2_mixer(hn, hgrn_w_in[j], lbs[layer], hgrn_norm_g[j], hgrn_w_out[j])
        h = h + y.astype(h.dtype)
    return rms_norm_2(h, final_g)


def setup_inputs(seed=0):
    out = dict(first_inputs(seed))
    for name, value in second_inputs(seed + 1).items():
        if name != "x":
            out[name + "_2"] = value
    return out


def reference(
    x, c, positions, w_ada, b_ada, g_pre_mix, g_post_mix, w_in, conv_w, w_out, g_pre_mlp,
    g_post_mlp, w_fc1, w_fc2, norm_g_2, pool_w_in_2, pool_w_grp_2, pool_scale_2, pool_w_out_2,
    hgrn_w_in_2, hgrn_lower_bounds_2, hgrn_norm_g_2, hgrn_w_out_2, final_g_2,
):
    x = first_block(
        x, c, positions, w_ada, b_ada, g_pre_mix, g_post_mix, w_in, conv_w, w_out, g_pre_mlp,
        g_post_mlp, w_fc1, w_fc2,
    )
    return second_block(
        x, norm_g_2, pool_w_in_2, pool_w_grp_2, pool_scale_2, pool_w_out_2, hgrn_w_in_2,
        hgrn_lower_bounds_2, hgrn_norm_g_2, hgrn_w_out_2, final_g_2,
    )


_drawn_inputs = setup_inputs


def setup_inputs(seed=0):
    import zlib

    import numpy as np

    out = dict(_drawn_inputs(seed))
    spreads = {}
    factors = {'g_post_mlp': 2.766, 'hgrn_norm_g_2': 2.892}
    for name, (base, spread) in spreads.items():
        noise = np.random.default_rng([zlib.crc32(name.encode()), seed]).standard_normal(out[name].shape)
        drawn = base * np.exp(spread * noise) if base else spread * noise
        out[name] = __import__('jax').numpy.asarray(drawn.astype(out[name].dtype))
    for name, factor in factors.items():
        out[name] = (out[name] * factor).astype(out[name].dtype)
    return out
```

```python
from contextlib import ExitStack

import concourse.bass as bass
import numpy as np
from concourse import mybir

F32 = mybir.dt.float32
F32R = mybir.dt.float32r
I32 = mybir.dt.int32
U8 = mybir.dt.uint8
ALU = mybir.AluOpType
ACT = mybir.ActivationFunctionType

T = 512
EPS = 1e-6
NR = 6
NS = 4
NZ = 3

V_C, V_BADA, V_GPRE1, V_GPOST1, V_GPRE2, V_GPOST2 = 0, 8, 56, 64, 72, 80
V_CONV, V_NG0, V_NG1, V_FG, V_PS, V_LB, V_HG, V_N = 88, 100, 108, 116, 124, 140, 172, 188
C_ID, C_FREQ, C_SGN, C_HPI, C_CNT, C_D = 0, 128, 129, 130, 131, 195
C_N = 195 + 4 * T


def unit_list():
    out = [("ada", n, False) for n in range(16)]
    ada = iter(range(16, 48))
    for n in range(28):
        out.append(("w_in", n, True))
        n_ada = 1 if n < 24 else 2
        out += [("ada", m, False) for _, m in zip(range(n_ada), ada)]
    for name, n in (("w_out", 8), ("w_fc1", 32), ("w_fc2", 32), ("pool_in", 40), ("pool_out", 16),
                    ("hgrn_in", 64), ("hgrn_out", 16)):
        out += [(name, i, True) for i in range(n)]
    return out


class Queue:

    def __init__(self, sem):
        self.sem, self.count, self.items, self.seen = sem, 0, [], {}

    def put(self, fn, *waits):
        todo = []
        for m in waits:
            if m is None:
                continue
            sem, value = m
            if self.seen.get(id(sem), 0) < value:
                self.seen[id(sem)] = value
                todo.append((sem, value))
        self.count += 1
        self.items.append((todo, fn))
        return self.sem, self.count

    def emit(self, eng):
        for todo, fn in self.items:
            for sem, value in todo:
                eng.wait_ge(sem, value)
            fn(eng).then_inc(self.sem, 1)


def build(nc, a):
    with ExitStack() as ctx:
        def sb(name, shape, dt=F32):
            return ctx.enter_context(nc.sbuf_tensor(name, shape, dt))

        def sem(name):
            return ctx.enter_context(nc.semaphore(name))

        X = sb("X", [128, 8, T])
        HH = sb("HH", [128, 8, T], F32R)
        HL = sb("HL", [128, 8, T], F32R)
        RAW = sb("RAW", [128, NR, 1024])
        WH = sb("WH", [128, NS, 1024], F32R)
        WL = sb("WL", [128, NS, 1024], F32R)
        Z = sb("Z", [128, 32, T])
        ZH = sb("ZH", [128, NZ, T], F32R)
        ZL = sb("ZL", [128, NZ, T], F32R)
        VEC = sb("VEC", [128, V_N])
        CST = sb("CST", [128, C_D])
        MSK = sb("MSK", [128, 6 * 256], U8)
        ONES = sb("ONES", [128, 128])
        MOD = sb("MOD", [128, 48])
        COL = sb("COL", [128, 96])
        RB = sb("RB", [128, T])
        DG = sb("DG", [128, T])
        TMP = sb("TMP", [128, 5, T])
        NW = sb("NW", [128, 6, 16])
        NWI = sb("NWI", [128, 2, 16], I32)
        PS = [ctx.enter_context(nc.psum_tensor(f"PS{i}", [128, T], F32)) for i in range(8)]

        s_raw = [sem(f"s_raw{i}") for i in range(NR)]
        s_vec, s_cst, s_x, s_pos, s_d, s_msk, s_out = (
            sem(n) for n in ("s_vec", "s_cst", "s_x", "s_pos", "s_d", "s_msk", "s_out"))
        PE, DV, AC, PO = (Queue(sem(n)) for n in ("s_pe", "s_dve", "s_act", "s_pool"))
        sp = []

        units = unit_list()
        split_of = [i for i, u in enumerate(units) if u[2]]
        freed = {}
        st = {"next": 0, "split": 0, "unit": 0, "z": 0, "ada": 0}
        w_ready, w_used = {}, {}

        def load_unit(i):
            name, n, _ = units[i]
            m = freed.get(i - NR)
            sp.append(([m] if m else [], RAW[:, i % NR, :], a[name][n], s_raw[i % NR]))

        def landed(i):
            return s_raw[i % NR], 16 * (i // NR + 1)

        ACC = Z[:, 26:28, :].rearrange("p a b -> p (a b)")
        ada = {"acc": None, "sum": None, "read": None}

        def sum_ada(i, n):
            j, k = divmod(n, 8)
            src = RAW[:, i % NR, :]
            sc = COL[:, k:k + 1]
            if k == 0:
                m = DV.put(lambda e: e.tensor_scalar(ACC, src, sc, None, ALU.mult),
                           landed(i), silu_c, ada["read"])
            else:
                m = DV.put(lambda e: e.scalar_tensor_tensor(out=ACC, in0=src, scalar=sc, in1=ACC,
                                                            op0=ALU.mult, op1=ALU.add),
                           landed(i), ada["acc"])
            ada["acc"] = m
            if k == 7:
                def mm(e):
                    for c in range(8):
                        r = e.matmul(PS[7][:, 16 + c:17 + c], ACC[:, 128 * c:128 * c + 128], ONES[:, 0:1],
                                     start=True, stop=True)
                    return r
                ada["read"] = PE.put(mm, m, ada["sum"], small["free"])
                ada["sum"] = DV.put(
                    lambda e: e.tensor_tensor(MOD[:, 8 * j:8 * j + 8], PS[7][:, 16:24],
                                              VEC[:, V_BADA + 8 * j:V_BADA + 8 * j + 8], ALU.add),
                    ada["read"])
                small["free"] = ada["sum"]
                mod[j] = ada["sum"]
            return m

        def advance():
            i = st["next"]
            if i >= len(units):
                return
            st["next"] += 1
            name, n, split = units[i]
            if split:
                s = st["split"]
                st["split"] += 1
                slot = s % NS
                hi = AC.put(lambda e: e.activation(WH[:, slot, :], RAW[:, i % NR, :], ACT.Copy),
                            landed(i), w_used.get(s - NS))
                freed[i] = w_ready[s] = DV.put(
                    lambda e: e.tensor_tensor(WL[:, slot, :], RAW[:, i % NR, :],
                                              WH[:, slot, :].bitcast(F32), ALU.subtract), hi)
            else:
                freed[i] = sum_ada(i, n)
            if i + NR < len(units):
                load_unit(i + NR)

        def unit():
            s = st["unit"]
            st["unit"] += 1
            while st["split"] < min(s + 3, len(split_of)):
                advance()
            return s, s % NS

        mod, small = {}, {"free": None}
        bank_free = [None] * 8

        def three(e, out, wh, wl, xh, xl, first, last):
            e.matmul(out, wh, xh, start=first, stop=False)
            e.matmul(out, wh, xl, start=False, stop=False)
            return e.matmul(out, wl, xh, start=False, stop=last)

        def gemm4(banks, tokens, h_ready, evac):
            for q in range(4):
                s, slot = unit()
                wh = WH[:, slot, :].rearrange("p (k c) -> p k c", k=2)
                wl = WL[:, slot, :].rearrange("p (k c) -> p k c", k=2)
                for kk in range(2):
                    k = 2 * q + kk
                    for j in range(4):
                        cols = slice(128 * j, 128 * j + 128)

                        def mm(e, j=j, k=k, kk=kk, cols=cols, wh=wh, wl=wl):
                            if tokens:
                                return three(e, PS[banks[j]][:, :], HH[:, k, cols], HL[:, k, cols],
                                             wh[:, kk, :], wl[:, kk, :], k == 0, k == 7)
                            return three(e, PS[banks[j]][:, :], wh[:, kk, cols], wl[:, kk, cols],
                                         HH[:, k, :], HL[:, k, :], k == 0, k == 7)
                        m = PE.put(mm, w_ready[s], h_ready[k], bank_free[banks[j]] if k == 0 else None)
                        if k == 7:
                            evac(j, m)
                    yield
                w_used[s] = m

        def gemm1(bank, h_ready, evac, nk=8):
            s, slot = unit()
            for k in range(nk):
                cols = slice(128 * k, 128 * k + 128)
                m = PE.put(lambda e, k=k, cols=cols: three(
                    e, PS[bank][:, :], WH[:, slot, cols], WL[:, slot, cols], HH[:, k, :], HL[:, k, :],
                    k == 0, k == 7), w_ready[s], h_ready[k], bank_free[bank] if k == 0 else None)
                if k == 7:
                    w_used[s] = m
                    evac(m)
                yield

        def run(main, *side):
            for _ in main:
                for g in side:
                    next(g, None)

        def split_z(src, n, ready):
            z = n % NZ
            hi = AC.put(lambda e: e.activation(ZH[:, z, :], src, ACT.Copy), ready, z_used.get(n - NZ))
            return DV.put(lambda e: e.tensor_tensor(ZL[:, z, :], src, ZH[:, z, :].bitcast(F32),
                                                    ALU.subtract), hi, ready)

        z_used = {}

        def gemm_out(nk, z_ready, evac):
            base = st["z"]
            st["z"] += nk
            ready = {}
            for k in range(min(2, nk)):
                ready[k] = split_z(Z[:, k, :], base + k, z_ready[k])
            for k in range(nk):
                s, slot = unit()
                if k + 2 < nk:
                    ready[k + 2] = split_z(Z[:, k + 2, :], base + k + 2, z_ready[k + 2])
                z = (base + k) % NZ
                for f in range(8):
                    cols = slice(128 * f, 128 * f + 128)
                    m = PE.put(lambda e, f=f, k=k, cols=cols, z=z, slot=slot: three(
                        e, PS[f][:, :], WH[:, slot, cols], WL[:, slot, cols], ZH[:, z, :], ZL[:, z, :],
                        k == 0, k == nk - 1), w_ready[s], ready[k], bank_free[f] if k == 0 else None)
                    if k == nk - 1:
                        evac(f, m)
                w_used[s] = z_used[base + k] = m

        def column_sums(src, col, ready, first=True, last=True):
            def mm(e):
                for j in range(4):
                    r = e.matmul(PS[7][:, col + j:col + j + 1], src[:, 128 * j:128 * j + 128], ONES[:, 0:1],
                                 start=first and j == 0, stop=last, skip_group_check=True)
                return r
            return PE.put(mm, ones, ready, small["free"] if first else None, bank_free[7] if first else None)

        def rsqrt(n, scale, ready):
            x, y, t, xh = (NW[:, i, 0:n] for i in range(4))
            i0, i1 = NWI[:, 0, 0:n], NWI[:, 1, 0:n]
            m = DV.put(lambda e: e.tensor_scalar(x, PS[7][:, 0:n], scale, EPS, ALU.mult, ALU.add),
                       ready, nw["used"])
            small["free"] = m
            m1 = DV.put(lambda e: e.tensor_scalar(xh, x, -0.5, None, ALU.mult), m)
            m = DV.put(lambda e: e.tensor_single_scalar(i0, x.bitcast(I32), 1, ALU.logical_shift_right), m)
            m = DV.put(lambda e: e.tensor_scalar(i1, i0, -1.0, 1597463007.0, ALU.mult, ALU.add), m)
            cur = i1.bitcast(F32)
            for it in range(4):
                src = cur
                m = DV.put(lambda e, src=src: e.tensor_tensor(t, src, src, ALU.mult), m)
                m = DV.put(lambda e: e.tensor_tensor(t, t, xh, ALU.mult), m, m1)
                dst = NW[:, 0, 0:n] if it % 2 else y
                m = DV.put(lambda e, src=src, dst=dst: e.scalar_tensor_tensor(
                    out=dst, in0=t, scalar=1.5, in1=src, op0=ALU.add, op1=ALU.mult), m)
                cur = dst
            return m

        nw = {"used": None}

        def spread(c0, bank, ready):
            m = ready
            for j in range(4):
                m = DV.put(lambda e, j=j: e.tensor_scalar(
                    DG[:, 128 * j:128 * j + 128], IDN, NW[:, 0, c0 + j:c0 + j + 1], None, ALU.mult),
                    ready, dg["used"])
            nw["used"] = m

            def mm(e):
                for j in range(4):
                    r = e.matmul(PS[bank][:, 128 * j:128 * j + 128], ONES[:, :],
                                 DG[:, 128 * j:128 * j + 128], start=True, stop=True)
                return r
            m = PE.put(mm, m, bank_free[bank])
            dg["used"] = m
            return m

        dg = {"used": None}
        rb = {"used": None}

        def factors(ready):
            m = spread(0, 6, rsqrt(4, 1.0 / 1024, ready))
            m = AC.put(lambda e: e.activation(RB[:, :], PS[6][:, :], ACT.Copy), m, rb["used"])
            bank_free[6] = m
            return m

        tmp_free = [None] * 5
        h_used = {"m": None}

        def make_h(gain, shift, x_ready, ready):
            out = []
            for k in range(8):
                t = TMP[:, k % 2, :]
                m = DV.put(lambda e, k=k, t=t: e.scalar_tensor_tensor(
                    out=t, in0=X[:, k, :], scalar=gain[:, k:k + 1], in1=RB[:, :], op0=ALU.mult,
                    op1=ALU.mult), ready, x_ready[k], tmp_free[k % 2])
                if shift is None:
                    hi = AC.put(lambda e, k=k, t=t: e.activation(HH[:, k, :], t, ACT.Copy), m, h_used["m"])
                    m = DV.put(lambda e, k=k, t=t: e.tensor_tensor(
                        HL[:, k, :], t, HH[:, k, :].bitcast(F32), ALU.subtract), hi)
                else:
                    hi = AC.put(lambda e, k=k, t=t: e.activation(
                        HH[:, k, :], t, ACT.Identity, bias=shift[:, k:k + 1]), m, h_used["m"])
                    m = DV.put(lambda e, k=k, t=t: e.scalar_tensor_tensor(
                        out=HL[:, k, :], in0=t, scalar=shift[:, k:k + 1], in1=HH[:, k, :].bitcast(F32),
                        op0=ALU.add, op1=ALU.subtract), hi)
                tmp_free[k % 2] = m
                out.append(m)
            rb["used"] = m
            return out

        IDN = CST[:, C_ID:C_ID + 128]

        sp.append(([], VEC[:, :], a["vec"], s_vec))
        sp.append(([], CST[:, :], a["cst"][:, 0:C_D], s_cst))
        POSI = Z[:, 31, :].bitcast(I32)
        sp.append(([], POSI, a["positions"].partition_broadcast(128), s_pos))
        sp.append(([], X[:, :, :], a["x"].rearrange("(k p) t -> p k t", p=128), s_x))
        vec, cst, x_in = (s_vec, 16), (s_cst, 16), (s_x, 16)
        for i in range(NR):
            load_unit(i)
        DMASK = Z[:, 22:26, :]
        sp.append(([], DMASK, a["cst"][:, C_D:C_N].rearrange("p (h t) -> p h t", h=4), s_d))
        sp.append(([], Z[:, 0:3, :].rearrange("p a b -> p (a b)"), a["msk"], s_msk))

        ones = DV.put(lambda e: e.memset(ONES[:, :], 1.0))
        m = AC.put(lambda e: e.activation(COL[:, 8:16], VEC[:, V_C:V_C + 8], ACT.Sigmoid), vec)
        silu_c = DV.put(lambda e: e.tensor_tensor(COL[:, 0:8], COL[:, 8:16], VEC[:, V_C:V_C + 8],
                                                  ALU.mult), m, ones)

        def square_sums(src, ready, k, last=7):
            t = TMP[:, 2 + k % 2, :]
            m = AC.put(lambda e: e.activation(t, src, ACT.Square), ready, tmp_free[2 + k % 2])
            m = column_sums(t, 0, m, first=k == 0, last=k == last)
            tmp_free[2 + k % 2] = m
            return m

        for k in range(8):
            m = square_sums(X[:, k, :], x_in, k)
        r1 = factors(m)

        ANG, TN, COS, SIN = Z[:, 30, :], Z[:, 29, :], Z[:, 20, :], Z[:, 21, :]
        m = DV.put(lambda e: e.tensor_copy(TN, POSI), (s_pos, 16))
        m = DV.put(lambda e: e.tensor_scalar(ANG, TN, CST[:, C_FREQ:C_FREQ + 1], None, ALU.mult), m, cst)
        m = DV.put(lambda e: e.tensor_scalar(TN, ANG, float(np.float32(1 / (2 * np.pi))), 12582912.0,
                                             ALU.mult, ALU.add), m)
        m = DV.put(lambda e: e.tensor_scalar(TN, TN, 12582912.0, None, ALU.subtract), m)
        for part in TWO_PI:
            m = DV.put(lambda e, part=part: e.scalar_tensor_tensor(
                out=ANG, in0=TN, scalar=-part, in1=ANG, op0=ALU.mult, op1=ALU.add), m)
        msin = AC.put(lambda e: e.activation(SIN, ANG, ACT.Sin, scale=0.5), m)
        m = DV.put(lambda e: e.scalar_tensor_tensor(
            out=TN, in0=ANG, scalar=-1.0, in1=ANG, op0=ALU.mult, op1=ALU.max), m)
        m = AC.put(lambda e: e.activation(COS, TN, ACT.Sin, scale=-0.5, bias=CST[:, C_HPI:C_HPI + 1]), m)
        m1 = DV.put(lambda e: e.tensor_tensor(TN, SIN, SIN, ALU.mult), msin, m)
        m = DV.put(lambda e: e.scalar_tensor_tensor(out=SIN, in0=SIN, scalar=CST[:, C_SGN:C_SGN + 1],
                                                    in1=COS, op0=ALU.mult, op1=ALU.mult), m1)
        rot = DV.put(lambda e: e.tensor_scalar(COS, TN, -2.0, 1.0, ALU.mult, ALU.add), m)

        for _ in range(16):
            advance()
        GA = COL[:, 16:24]
        m = DV.put(lambda e: e.scalar_tensor_tensor(
            out=GA, in0=MOD[:, 8:16], scalar=1.0, in1=VEC[:, V_GPRE1:V_GPRE1 + 8], op0=ALU.add,
            op1=ALU.mult), mod[1])
        m = DV.put(lambda e: e.tensor_copy(COL[:, 24:32], MOD[:, 0:8]), m, mod[0])
        h_ready = make_h(GA, COL[:, 24:32], [x_in] * 8, DV.put(
            lambda e: e.tensor_copy(COL[:, 32:33], COL[:, 16:17]), m, r1))

        masks = DV.put(lambda e: e.tensor_copy(MSK[:, :], Z[:, 0:3, :].rearrange("p a b -> p (a b)")),
                       (s_msk, 16))

        z_ready = [None] * 32
        v_ready = [None] * 4
        VT = Z[:, 16:20, :]

        def evac_v(j, m):
            v_ready[j] = AC.put(lambda e: e.activation(VT[:, j, :], PS[j][:, :], ACT.Copy), m)
            bank_free[j] = v_ready[j]
        run(gemm4([0, 1, 2, 3], True, h_ready, evac_v))

        def temp(i, fn, eng, *waits):
            m = eng.put(fn, tmp_free[i], *waits)
            return m

        qk_ready = [None] * 8

        def evac_rot(n, bank):
            def go(m):
                ps, b, out = PS[bank], TMP[:, n % 2, :], Z[:, 8 + n, :]
                DV.put(lambda e: e.tensor_tensor(b[0:64, :], ps[64:128, :], SIN[0:64, :], ALU.mult),
                       m, rot, tmp_free[n % 2])
                m1 = DV.put(lambda e: e.tensor_tensor(b[64:128, :], ps[0:64, :], SIN[64:128, :], ALU.mult), m)
                m2 = DV.put(lambda e: e.tensor_tensor(out, ps[:, :], COS, ALU.mult), m)
                bank_free[bank] = m2
                m = DV.put(lambda e: e.tensor_tensor(out, out, b, ALU.add), m1, m2)
                tmp_free[n % 2] = qk_ready[n] = m
            return go

        def evac_silu(dst, bank, done):
            def go(m):
                m = AC.put(lambda e: e.activation(dst, PS[bank][:, :], ACT.Sigmoid), m)
                m = DV.put(lambda e: e.tensor_tensor(dst, dst, PS[bank][:, :], ALU.mult), m)
                bank_free[bank] = m
                done(m)
            return go

        ring = [4, 5, 6]
        nb = 0
        for n in range(8):
            run(gemm1(ring[nb % 3], h_ready, evac_rot(n, ring[nb % 3])))
            nb += 1
        sg_ready = [None] * 4
        for n in range(4):
            def done(m, n=n):
                sg_ready[n] = m
            run(gemm1(ring[nb % 3], h_ready, evac_silu(Z[:, 4 + n, :], ring[nb % 3], done)))
            nb += 1

        def retention(h):
            A = Z[:, 28:31, :].rearrange("p a b -> p (a b)")
            off = [0, 512, 896, 1152]
            ready = []
            for i in range(4):
                n = T - 128 * i
                bank = i % 2
                m = PE.put(lambda e, i=i, n=n, bank=bank: e.matmul(
                    PS[bank][:, 0:n], Z[:, 12 + h, 128 * i:128 * i + 128], Z[:, 8 + h, 128 * i:T],
                    start=True, stop=True), qk_ready[h], qk_ready[4 + h], bank_free[bank])
                m = DV.put(lambda e, i=i, n=n, bank=bank: e.tensor_tensor(
                    A[:, off[i]:off[i] + n], PS[bank][:, 0:n], DMASK[:, h, 0:n], ALU.mult),
                    m, (s_d, 16), ret["a"], rot)
                bank_free[bank] = m
                ready.append(m)
                yield
            ob = 2 + h % 2
            for i in range(4):
                n = T - 128 * i
                m = PE.put(lambda e, i=i, n=n: e.matmul(
                    PS[ob][:, 128 * i:T], VT[:, i, 128 * h:128 * h + 128], A[:, off[i]:off[i] + n],
                    start=i == 0, stop=i == 3), ready[i], v_ready[i], bank_free[ob])
                yield
            ret["a"] = m
            t = TMP[:, 2 + h % 2, :]
            m1 = AC.put(lambda e: e.activation(t, PS[ob][:, :], ACT.Square), m, tmp_free[2 + h % 2])
            m2 = DV.put(lambda e: e.tensor_tensor(Z[:, 4 + h, :], PS[ob][:, :], Z[:, 4 + h, :], ALU.mult),
                        m, sg_ready[h], m1)
            bank_free[ob] = m2
            yield
            ret["sum"] = column_sums(t, 4 * h, m1, first=True)
            tmp_free[2 + h % 2] = ret["sum"]
            ret["z"][h] = m2
            yield

        ret = {"a": None, "sum": None, "z": [None] * 4}

        def ret_norm():
            m = rsqrt(16, 1.0 / 128, ret["sum"])
            for h in range(4):
                bank = h % 2
                m1 = spread(4 * h, bank, m)
                z_ready[4 + h] = DV.put(lambda e, h=h, bank=bank: e.tensor_tensor(
                    Z[:, 4 + h, :], Z[:, 4 + h, :], PS[bank][:, :], ALU.mult), m1, ret["z"][h])
                bank_free[bank] = z_ready[4 + h]
                yield

        def chain(*gens):
            for g in gens:
                yield from g

        side = chain(*(retention(h) for h in range(4)), ret_norm())

        conv = {}

        def evac_x(i, bank):
            def go(m):
                conv["x"] = AC.put(lambda e: e.activation(TMP[:, 0, :], PS[bank][:, :], ACT.Copy),
                                   m, tmp_free[0])
                bank_free[bank] = conv["x"]
            return go

        def evac_c(i, bank):
            def go(m):
                u = TMP[:, 1, :]
                y = Z[:, i, :]
                w = [VEC[:, V_CONV + 4 * j + i:V_CONV + 4 * j + i + 1] for j in range(3)]
                m = DV.put(lambda e: e.tensor_tensor(u, TMP[:, 0, :], PS[bank][:, :], ALU.mult),
                           m, conv["x"], tmp_free[1])
                bank_free[bank] = tmp_free[0] = m
                m = DV.put(lambda e: e.tensor_scalar(y, u, w[2], None, ALU.mult), m)
                for j in (1, 2):
                    m = DV.put(lambda e, j=j: e.scalar_tensor_tensor(
                        out=y[:, j:T], in0=u[:, 0:T - j], scalar=w[2 - j], in1=y[:, j:T],
                        op0=ALU.mult, op1=ALU.add), m)
                tmp_free[1] = conv["y"] = m
            return go

        def evac_b(i, bank):
            def go(m):
                z_ready[i] = DV.put(lambda e: e.tensor_tensor(Z[:, i, :], Z[:, i, :], PS[bank][:, :],
                                                              ALU.mult), m, conv["y"])
                bank_free[bank] = z_ready[i]
            return go

        for i in range(4):
            for ev in (evac_x, evac_c, evac_b):
                run(gemm1(ring[nb % 3], h_ready, ev(i, ring[nb % 3])), side)
                nb += 1
        for _ in side:
            pass
        h_used["m"] = (PE.sem, PE.count)
        while st["split"] < 31:
            advance()

        def gains(dst, j, g, one):
            return DV.put(lambda e: e.scalar_tensor_tensor(
                out=COL[:, dst:dst + 8], in0=MOD[:, 8 * j:8 * j + 8], scalar=1.0 if one else 0.0,
                in1=VEC[:, g:g + 8], op0=ALU.add, op1=ALU.mult), mod[j])

        def residual(nk, z_ready, gate, gate_ready, x_ready):
            y_ready = []
            box = {}

            def evac(f, m):
                y = AC.put(lambda e: e.activation(Z[:, f, :], PS[f][:, :], ACT.Copy), m)
                bank_free[f] = y
                y_ready.append(y)
            gemm_out(nk, z_ready, evac)
            for f in range(8):
                t = TMP[:, 2 + f % 2, :]
                m = DV.put(lambda e, f=f, t=t: e.tensor_tensor(t, Z[:, f, :], Z[:, f, :], ALU.mult),
                           y_ready[f], tmp_free[2 + f % 2])
                m = column_sums(t, 0, m, first=f == 0, last=f == 7)
                tmp_free[2 + f % 2] = m
            r = factors(m)
            out = []
            for f in range(8):
                t = TMP[:, f % 2, :]
                m = DV.put(lambda e, f=f, t=t: e.scalar_tensor_tensor(
                    out=t, in0=Z[:, f, :], scalar=gate[:, f:f + 1], in1=RB[:, :], op0=ALU.mult,
                    op1=ALU.mult), r, gate_ready, tmp_free[f % 2])
                m = DV.put(lambda e, f=f, t=t: e.tensor_tensor(X[:, f, :], X[:, f, :], t, ALU.add),
                           m, x_ready[f])
                tmp_free[f % 2] = m
                out.append(m)
                m = square_sums(X[:, f, :], m, f)
            rb["used"] = out[-1]
            return out, factors(m)

        g1 = gains(32, 2, V_GPOST1, False)
        g2 = gains(40, 4, V_GPRE2, True)
        g3 = gains(48, 5, V_GPOST2, False)
        b2 = DV.put(lambda e: e.tensor_copy(COL[:, 56:64], MOD[:, 24:32]), mod[3])
        x_ready, r = residual(8, z_ready, COL[:, 32:40], g1, [x_in] * 8)

        m = DV.put(lambda e: e.tensor_copy(COL[:, 64:65], COL[:, 40:41]), g2, g3, b2)
        h_ready = make_h(COL[:, 40:48], COL[:, 56:64], x_ready, r)

        def evac_relu(f, bank):
            def go(m):
                t = TMP[:, f % 2, :]
                m = AC.put(lambda e: e.activation(t, PS[bank][:, :], ACT.Relu), m, tmp_free[f % 2])
                bank_free[bank] = m
                z_ready[f] = tmp_free[f % 2] = DV.put(
                    lambda e: e.tensor_tensor(Z[:, f, :], t, t, ALU.mult), m)
            return go
        run(gemm4([0, 1, 2, 3], False, h_ready, lambda j, m: evac_relu(j, j)(m)))
        for f in range(4, 32):
            bank = f % 8
            run(gemm1(bank, h_ready, evac_relu(f, bank)))
        h_used["m"] = (PE.sem, PE.count)
        x_ready, r = residual(32, z_ready, COL[:, 48:56], g3, x_ready)

        h_ready = make_h(VEC[:, V_NG0:V_NG0 + 8], None, x_ready, r)
        PADW = 16 + T
        flat = Z[:, 20:32, :].rearrange("p a b -> p (a b)")
        VP, S1, S2, PP = (flat[:, PADW * i:PADW * (i + 1)] for i in range(4))
        pads = DV.put(lambda e: e.memset(flat[:, 0:4 * PADW], 0.0), r, (PE.sem, PE.count))
        pool = {"free": pads, "p": {}, "g": {}}

        def window(g, j, bank):
            def go(m):
                w = 2 << g
                m = AC.put(lambda e: e.activation(VP[:, 16:PADW], PS[bank][:, :], ACT.Copy),
                           m, pool["free"])
                bank_free[bank] = m
                src, dst = VP, S1
                for lev in range(g + 1):
                    sh = 1 << lev
                    m = DV.put(lambda e, src=src, dst=dst, sh=sh: e.tensor_tensor(
                        dst[:, 16:PADW], src[:, 16:PADW], src[:, 16 - sh:PADW - sh], ALU.add), m)
                    src, dst = dst, (S2 if dst is S1 else S1)
                p = PP[:, 0:T]
                m1 = DV.put(lambda e: e.scalar_tensor_tensor(
                    out=p[:, 16:T], in0=src[:, 32:PADW], scalar=1.0 / w, in1=VP[:, 32:PADW],
                    op0=ALU.mult, op1=ALU.subtract), m)
                m2 = DV.put(lambda e: e.tensor_tensor(
                    p[:, 0:16], src[:, 16:32], CST[:, C_CNT + 16 * g:C_CNT + 16 * g + 16], ALU.mult), m)
                m = DV.put(lambda e: e.tensor_tensor(p[:, 0:16], p[:, 0:16], VP[:, 16:32], ALU.subtract), m2)
                hi = AC.put(lambda e: e.activation(PHI(j), p, ACT.Copy), m, m1, grp["used"])
                m = DV.put(lambda e: e.tensor_tensor(PLO(j), p, PHI(j).bitcast(F32), ALU.subtract), hi)
                pool["free"] = m
                pool["p"][j] = m
            return go

        scope = ctx.enter_context(ExitStack())
        PSP = scope.enter_context(nc.sbuf_tensor("PSP", [128, 4, T], F32R))

        def PHI(j):
            return PSP[:, j, :]

        def PLO(j):
            return (ZH if j < 3 else ZL)[:, j % 3, :]
        grp = {"used": (PE.sem, PE.count)}
        for g in range(4):
            if g == 0:
                run(gemm4([0, 1, 2, 3], False, h_ready, lambda j, m: window(0, j, j)(m)))
            else:
                for j in range(4):
                    run(gemm1(j, h_ready, window(g, j, j)))
            for j in range(4):
                def done(m, j=j):
                    pool["g"][j] = m
                run(gemm1(4 + j, h_ready, evac_silu(Z[:, 16 + j, :], 4 + j, done)))
            for q in range(2):
                s, slot = unit()
                wh = WH[:, slot, :].rearrange("p (k c) -> p k c", k=4)
                wl = WL[:, slot, :].rearrange("p (k c) -> p k c", k=4)
                for i in range(2):
                    f = 2 * q + i
                    bank = f
                    cols = slice(128 * i, 128 * i + 128)
                    for k in range(4):
                        m = PE.put(lambda e, k=k, bank=bank, cols=cols, wh=wh, wl=wl: three(
                            e, PS[bank][:, :], wh[:, k, cols], wl[:, k, cols], PHI(k), PLO(k),
                            k == 0, k == 3), w_ready[s], pool["p"][k], bank_free[bank] if k == 0 else None)
                    zt = 4 * g + f
                    z_ready[zt] = DV.put(lambda e, zt=zt, f=f, bank=bank: e.scalar_tensor_tensor(
                        out=Z[:, zt, :], in0=PS[bank][:, :], scalar=VEC[:, V_PS + zt:V_PS + zt + 1],
                        in1=Z[:, 16 + f, :], op0=ALU.mult, op1=ALU.mult), m, pool["g"][f])
                    bank_free[bank] = z_ready[zt]
                w_used[s] = m
            grp["used"] = m
        h_used["m"] = (PE.sem, PE.count)

        def add_out(nk, x_ready):
            out = []

            def evac(f, m):
                m = DV.put(lambda e: e.tensor_tensor(X[:, f, :], X[:, f, :], PS[f][:, :], ALU.add),
                           m, x_ready[f])
                bank_free[f] = m
                out.append(m)
            for i in range(3):
                z_used[st["z"] - 1 - i] = grp["used"]
            gemm_out(nk, z_ready, evac)
            for f in range(8):
                m = square_sums(X[:, f, :], out[f], f)
            return out, factors(m)

        x_ready, r = add_out(16, x_ready)

        h_ready = make_h(VEC[:, V_NG1:V_NG1 + 8], None, x_ready, r)
        L0, L1 = VEC[:, V_LB:V_LB + 16], VEC[:, V_LB + 16:V_LB + 32]
        E0, E1, MX = NW[:, 4, :], NW[:, 5, :], NW[:, 3, :]
        LBC, OMC = COL[:, 0:16], COL[:, 16:32]
        last = (DV.sem, DV.count)
        m = DV.put(lambda e: e.tensor_tensor(MX, L0, L1, ALU.max), last)
        m1 = DV.put(lambda e: e.tensor_tensor(E0, L0, MX, ALU.subtract), m)
        m2 = DV.put(lambda e: e.tensor_tensor(E1, L1, MX, ALU.subtract), m)
        m1 = AC.put(lambda e: e.activation(E0, E0, ACT.Exp), m1, m2)
        m2 = AC.put(lambda e: e.activation(E1, E1, ACT.Exp), m2)
        m = DV.put(lambda e: e.tensor_tensor(MX, E0, E1, ALU.add), m1, m2)
        m = DV.put(lambda e: e.reciprocal(MX, MX), m)
        m1 = DV.put(lambda e: e.tensor_tensor(E0, E0, MX, ALU.mult), m)
        m2 = DV.put(lambda e: e.tensor_tensor(E1, E1, MX, ALU.mult), m)
        m = DV.put(lambda e: e.tensor_tensor(MX, E0, E1, ALU.add), m1, m2)
        m = DV.put(lambda e: e.tensor_tensor(LBC, MX, E0, ALU.subtract), m)
        lb_ready = DV.put(lambda e: e.tensor_scalar(OMC, LBC, -1.0, 1.0, ALU.mult, ALU.add), m)
        nw["used"] = lb_ready

        hv_ready = [None] * 16
        z_last = (PE.sem, PE.count)
        for g in range(4):
            banks = [0, 1, 2, 3] if g % 2 == 0 else [4, 5, 6, 7]

            def evac_hv(j, m, g=g, banks=banks):
                m = AC.put(lambda e: e.activation(
                    Z[:, 4 * g:4 * g + 4, 128 * j:128 * j + 128],
                    PS[banks[j]][:, :].rearrange("p (h v) -> p h v", h=4), ACT.Copy), m, z_last)
                bank_free[banks[j]] = m
                for h in range(4):
                    hv_ready[4 * g + h] = m
            run(gemm4(banks, True, h_ready, evac_hv))

        hflat = Z[:, 16:32, :].rearrange("p a b -> p (a b)")
        HB = 3968

        class Head:
            def __init__(self, b):
                at = [HB * b]

                def take(n):
                    at[0] += n
                    return hflat[:, at[0] - n:at[0]]
                self.q, self.f, self.k, self.sg = (take(T) for _ in range(4))
                self.tot = take(T)
                self.ad, self.ax = take(T), take(768)
                self.free = None
        heads = [Head(0), Head(1)]
        scope.close()
        QP = [sb("QP0", [128, T]), sb("QP1", [128, T])]
        LVB, OB, RBK = [3, 4], 5, 6
        hz = [None] * 16
        lv = {"n": 0}

        def project(h):
            b = heads[h % 2]
            col = slice(h, h + 1)

            def ev_q(m):
                b.q_ready = AC.put(lambda e: e.activation(b.q, PS[0][:, :], ACT.Copy), m, b.free)
                bank_free[0] = b.q_ready

            def ev_f(m):
                m1 = AC.put(lambda e: e.activation(b.f, PS[1][:, :], ACT.Sigmoid), m, b.free)
                m2 = AC.put(lambda e: e.activation(b.k, PS[1][:, :], ACT.Sigmoid, scale=-1.0), m)
                bank_free[1] = m2
                m1 = DV.put(lambda e: e.tensor_scalar(b.f, b.f, OMC[:, col], LBC[:, col], ALU.mult,
                                                      ALU.add), m1, lb_ready)
                b.k_ready = DV.put(lambda e: e.tensor_scalar(b.k, b.k, OMC[:, col], None, ALU.mult), m2)
                b.f_ready = m1
                b.qp_ready = DV.put(lambda e: e.tensor_tensor(QP[h % 2][:, :], b.q, b.f, ALU.mult),
                                    m1, b.q_ready)

            def done(m):
                b.sg_ready = m
            yield from gemm1(0, h_ready, ev_q)
            yield from gemm1(1, h_ready, ev_f)
            yield from gemm1(2, h_ready, evac_silu(b.sg, 2, done))

        def mixing(h):
            b = heads[h % 2]
            qp = QP[h % 2]
            lvl = lambda: LVB[lv["n"] % 2]
            ad4 = b.ad.rearrange("p (i t) -> p i t", i=4)
            idn4 = IDN.rearrange("p (o t) -> p o t", o=1).broadcast_to([128, 4, 128])
            bank = lvl()
            lv["n"] += 1

            def mm(e, bank=bank):
                for i in range(4):
                    c = slice(128 * i, 128 * i + 128)
                    r = e.matmul(PS[bank][:, c], b.k[:, c], b.q[:, c], start=True, stop=True)
                return r
            m = PE.put(mm, b.k_ready, b.q_ready, bank_free[bank])
            a_ready = DV.put(lambda e, bank=bank: e.tensor_tensor(
                ad4, PS[bank][:, :].rearrange("p (i t) -> p i t", i=4), idn4, ALU.mult), m)
            bank_free[bank] = a_ready
            q_ready, k_ready, t_ready = b.qp_ready, b.k_ready, b.f_ready
            tot = b.f
            spare = [0]
            yield
            for lev in range(9):
                L = 1 << lev
                bank = lvl()
                lv["n"] += 1
                ps = PS[bank]
                if L <= 64:
                    rows = 128 if L < 64 else 64

                    def mm(e, L=L, ps=ps, rows=rows):
                        for i in range(4):
                            qv = qp[:, 128 * i:128 * i + 128].rearrange("p (n a l) -> p n a l", a=2, l=L)
                            o = ps[0:rows, 64 * i:64 * i + 64].rearrange("p (n l) -> p n l", l=L)
                            r = e.matmul(o, b.k[:, 128 * i:128 * i + rows], qv[:, :, 1, :],
                                         start=True, stop=True)
                        return r
                elif L == 128:
                    def mm(e, ps=ps):
                        for i in range(2):
                            r = e.matmul(ps[:, 128 * i:128 * i + 128], b.k[:, 256 * i:256 * i + 128],
                                         qp[:, 256 * i + 128:256 * i + 256], start=True, stop=True)
                        return r
                else:
                    def mm(e, ps=ps):
                        for i in range(2):
                            r = e.matmul(ps[:, 256 * i:256 * i + 256], b.k[:, 128 * i:128 * i + 128],
                                         qp[:, 256:512], start=True, stop=True)
                        return r
                used = PE.put(mm, q_ready, k_ready, bank_free[bank])
                if L < 256:
                    n = T // (2 * L)
                    tv = tot.rearrange("p (n a) -> p n a", a=2)
                    q2 = qp[:, :].rearrange("p (n a l) -> p n a l", a=2, l=L)[:, :, 1, :]
                    k2 = b.k.rearrange("p (n a l) -> p n a l", a=2, l=L)[:, :, 0, :]
                    q_ready = DV.put(lambda e, q2=q2, tv=tv, n=n, L=L: e.tensor_tensor(
                        q2, q2, tv[:, :, 0:1].broadcast_to([128, n, L]), ALU.mult), used, t_ready, q_ready)
                    k_ready = DV.put(lambda e, k2=k2, tv=tv, n=n, L=L: e.tensor_tensor(
                        k2, k2, tv[:, :, 1:2].broadcast_to([128, n, L]), ALU.mult), used, t_ready, k_ready)
                    if L < 128:
                        nt = b.tot[:, spare[0]:spare[0] + n]
                        spare[0] += n
                        t_ready = DV.put(lambda e, nt=nt, tv=tv: e.tensor_tensor(
                            nt, tv[:, :, 0], tv[:, :, 1], ALU.mult), t_ready)
                        tot = nt
                if L < 64:
                    n = T // (2 * L)
                    av = b.ad.rearrange("p (n a l) -> p n a l", a=2, l=L)[:, :, 1, :]
                    a_ready = DV.put(lambda e, av=av, ps=ps, lev=lev, L=L: e.copy_predicated(
                        av, MSK[:, 256 * lev:256 * lev + 256].rearrange("p (n l) -> p n l", l=L),
                        ps[:, 0:256].rearrange("p (n l) -> p n l", l=L)), used, a_ready, masks)
                    bank_free[bank] = a_ready
                elif L == 64:
                    a64 = AC.put(lambda e, ps=ps: e.activation(
                        ad4[0:64, :, 64:128], ps[0:64, 0:256].rearrange("p (i t) -> p i t", i=4),
                        ACT.Copy), used, a_ready)
                    bank_free[bank] = a64
                elif L == 128:
                    a128 = AC.put(lambda e, ps=ps: e.activation(b.ax[:, 0:256], ps[:, 0:256], ACT.Copy), used)
                    bank_free[bank] = a128
                else:
                    a256 = AC.put(lambda e, ps=ps: e.activation(b.ax[:, 256:768], ps[:, :], ACT.Copy), used)
                    bank_free[bank] = a256
                yield

            def pv(e):
                o, v = PS[OB], Z[:, h, :]
                for i in range(4):
                    c = slice(128 * i, 128 * i + 128)
                    e.matmul(o[:, c], v[:, c], b.ad[:, c], start=i == 0, stop=False, skip_group_check=True)
                for i in range(2):
                    e.matmul(o[:, 256 * i + 128:256 * i + 256], v[:, 256 * i:256 * i + 128],
                             b.ax[:, 128 * i:128 * i + 128], start=False, stop=False, skip_group_check=True)
                for i in range(2):
                    r = e.matmul(o[:, 256:512], v[:, 128 * i:128 * i + 128],
                                 b.ax[:, 256 + 256 * i:512 + 256 * i], start=False, stop=i == 1,
                                 skip_group_check=True)
                return r
            m = PE.put(pv, a64, a128, a256, hv_ready[h], bank_free[OB])
            b.free = m
            t = TMP[:, 2 + h % 2, :]
            m1 = AC.put(lambda e: e.activation(t, PS[OB][:, :], ACT.Square), m, tmp_free[2 + h % 2])
            hz[h] = DV.put(lambda e: e.scalar_tensor_tensor(
                out=Z[:, h, :], in0=PS[OB][:, :], scalar=VEC[:, V_HG + h:V_HG + h + 1], in1=b.sg,
                op0=ALU.mult, op1=ALU.mult), m, b.sg_ready, m1)
            bank_free[OB] = b.free = hz[h]
            yield
            m = column_sums(t, 4 * (h % 4), m1)
            tmp_free[2 + h % 2] = m
            if h % 4 == 3:
                yield
                m = rsqrt(16, 1.0 / 128, m)
                for i in range(4):
                    yield
                    m1 = spread(4 * i, RBK, m)
                    zt = h - 3 + i
                    z_ready[zt] = DV.put(lambda e, zt=zt: e.tensor_tensor(
                        Z[:, zt, :], Z[:, zt, :], PS[RBK][:, :], ALU.mult), m1, hz[zt])
                    bank_free[RBK] = z_ready[zt]
            yield

        for h in range(16):
            side = mixing(h - 1) if h else iter(())
            run(project(h), side)
            for _ in side:
                pass
        for _ in mixing(15):
            pass
        x_ready, r = add_out(16, x_ready)
        for f in range(8):
            m = DV.put(lambda e, f=f: e.scalar_tensor_tensor(
                out=Z[:, 16 + f, :], in0=X[:, f, :], scalar=VEC[:, V_FG + f:V_FG + f + 1], in1=RB[:, :],
                op0=ALU.mult, op1=ALU.mult), r, x_ready[f])
            sp.append(([m], a["out"][128 * f:128 * f + 128, :], Z[:, 16 + f, :], s_out))

        block = ctx.enter_context(nc.Block())

        @block.sync
        def _(e):
            for waits, dst, src, s in sp:
                for w in waits:
                    e.wait_ge(*w)
                e.dma_start(dst, src).then_inc(s, 16)
            e.wait_ge(s_out, 16 * 8)

        @block.tensor
        def _(e):
            PE.emit(e)

        @block.vector
        def _(e):
            DV.emit(e)

        @block.scalar
        def _(e):
            AC.emit(e)


def two_pi():
    rest, out = 2 * np.pi, []
    for _ in range(3):
        e = np.floor(np.log2(rest)) - 7
        part = np.floor(rest / 2.0 ** e) * 2.0 ** e
        out.append(float(part))
        rest -= part
    return out + [float(np.float32(rest))]


TWO_PI = two_pi()


def constants():
    c = np.zeros((128, C_N), np.float32)
    c[:, C_ID:C_ID + 128] = np.eye(128)
    half = np.arange(64, dtype=np.float32) / np.float32(64)
    c[:, C_FREQ] = np.tile((10000.0 ** -half.astype(np.float64)).astype(np.float32), 2)
    c[0:64, C_SGN], c[64:128, C_SGN] = -2.0, 2.0
    c[:, C_HPI] = np.pi / 2
    for g in range(4):
        c[:, C_CNT + 16 * g:C_CNT + 16 * g + 16] = 1.0 / np.minimum(np.arange(16) + 1.0, 2 << g)
    m, t = np.arange(128)[:, None], np.arange(T)[None, :]
    same = m // 64 == t // 64
    for h in range(4):
        gamma = 1.0 - 2.0 ** (-5.0 - h)
        d = np.where(same, gamma ** np.abs(t - m), np.where(t > m, gamma ** np.maximum(t - m, 0), 0.0))
        c[:, C_D + T * h:C_D + T * h + T] = d * 128.0 ** -0.5
    k = np.zeros((128, 6, 4, 64), np.float32)
    for lev in range(6):
        L = 1 << lev
        s, j = np.arange(128)[:, None], np.arange(64)[None, :]
        k[:, lev] = ((s // (2 * L) == j // L) & (s % (2 * L) < L))[:, None, :]
    return c, k.reshape(128, 6 * 256)


def columns(w):
    n = w.shape[1] // 128
    return w.reshape(8, 128, n, 128).transpose(2, 1, 0, 3).reshape(n, 128, 1024)


def groups(w):
    n = w.shape[1] // 512
    return w.reshape(4, 2, 128, n, 512).transpose(3, 0, 2, 1, 4).reshape(4 * n, 128, 1024)


def kernel(x, c, positions, w_ada, b_ada, g_pre_mix, g_post_mix, w_in, conv_w, w_out, g_pre_mlp,
           g_post_mlp, w_fc1, w_fc2, norm_g_2, pool_w_in_2, pool_w_grp_2, pool_scale_2, pool_w_out_2,
           hgrn_w_in_2, hgrn_lower_bounds_2, hgrn_norm_g_2, hgrn_w_out_2, final_g_2):
    import concourse.bacc as bacc
    from concourse.bass_utils import run_bass_kernel_spmd

    def col(v):
        return np.asarray(v).reshape(-1, 128).T

    cst, msk = constants()
    w1 = np.asarray(w_in)[0]
    q0 = 3 * 512
    order = [columns(w1[:, q0:q0 + 1024]), columns(w1[:, q0 + 1536:q0 + 2048])]
    parts = columns(w1[:, 0:1536])
    parts = parts[[3 * 0 + p * 4 + i - 0 for i in range(4) for p in (0, 2, 1)]]
    pin = np.asarray(pool_w_in_2)[0]
    grp = np.asarray(pool_w_grp_2)[0]
    pool = []
    for g in range(4):
        v = pin[:, 512 * g:512 * g + 512]
        pool.append(groups(v) if g == 0 else columns(v))
        pool.append(columns(pin[:, 2048 + 512 * g:2048 + 512 * g + 512]))
        pool.append(grp[g].reshape(4, 128, 2, 256).transpose(2, 1, 0, 3).reshape(2, 128, 1024))
    hin = np.asarray(hgrn_w_in_2)[0]
    qfg = np.stack([columns(hin[:, 0:2048]), columns(hin[:, 2048:4096]), columns(hin[:, 6144:8192])], 1)
    arrays = {
        "x": np.asarray(x)[0].T,
        "positions": np.asarray(positions),
        "vec": np.concatenate([
            col(c), col(b_ada), col(g_pre_mix), col(g_post_mix), col(g_pre_mlp), col(g_post_mlp),
            col(conv_w), col(norm_g_2), col(final_g_2), col(pool_scale_2), col(hgrn_lower_bounds_2),
            col(hgrn_norm_g_2)], 1),
        "cst": cst,
        "msk": msk,
        "ada": np.asarray(w_ada)[0].reshape(8, 128, 6, 1024).transpose(2, 0, 1, 3).reshape(48, 128, 1024),
        "w_in": np.concatenate([groups(w1[:, q0 + 1024:q0 + 1536]), *order, parts]),
        "w_out": np.asarray(w_out)[0].reshape(8, 128, 1024),
        "w_fc1": np.concatenate([groups(np.asarray(w_fc1)[0][:, 0:512]),
                                 columns(np.asarray(w_fc1)[0][:, 512:4096])]),
        "w_fc2": np.asarray(w_fc2)[0].reshape(32, 128, 1024),
        "pool_in": np.concatenate(pool),
        "pool_out": np.asarray(pool_w_out_2)[0].reshape(16, 128, 1024),
        "hgrn_in": np.concatenate([groups(hin[:, 4096:6144]), qfg.reshape(48, 128, 1024)]),
        "hgrn_out": np.asarray(hgrn_w_out_2)[0].reshape(16, 128, 1024),
    }
    arrays = {k: np.ascontiguousarray(v) for k, v in arrays.items()}
    nc = bacc.Bacc("TRN2", target_bir_lowering=False, num_devices=1)
    aps = {k: nc.dram_tensor(f"in_{k}", v.shape, mybir.dt.from_np(v.dtype), kind="ExternalInput").ap()
           for k, v in arrays.items()}
    aps["out"] = nc.dram_tensor("out", (1024, T), F32, kind="ExternalOutput").ap()
    build(nc, aps)
    r = run_bass_kernel_spmd(nc, [{f"in_{k}": v for k, v in arrays.items()}], core_ids=[0])
    return np.ascontiguousarray(r.results[0]["out"].T)[None]
```

```python
from contextlib import ExitStack

import concourse.bass as bass
import numpy as np
from concourse import mybir

F32 = mybir.dt.float32
F32R = mybir.dt.float32r
I32 = mybir.dt.int32
U8 = mybir.dt.uint8
ALU = mybir.AluOpType
ACT = mybir.ActivationFunctionType

T = 512
EPS = 1e-6
NR = 5
NS = 4
NZ = 3

V_C, V_BADA, V_GPRE1, V_GPOST1, V_GPRE2, V_GPOST2 = 0, 8, 56, 64, 72, 80
V_CONV, V_NG0, V_NG1, V_FG, V_PS, V_LB, V_HG, V_N = 88, 100, 108, 116, 124, 140, 172, 188
C_ID, C_FREQ, C_SGN, C_HPI, C_CNT, C_D = 0, 128, 129, 130, 131, 195
C_N = 195 + 4 * T


def unit_list():
    out = [("ada", 8 * j + k, False) for j in (1, 0) for k in range(8)]
    ada = iter(range(16, 48))
    for n in range(28):
        out.append(("w_in", n, True))
        n_ada = 1 if n < 24 else 2
        out += [("ada", m, False) for _, m in zip(range(n_ada), ada)]
    for name, n in (("w_out", 8), ("w_fc1", 32), ("w_fc2", 32), ("pool_in", 40), ("pool_out", 16),
                    ("hgrn_in", 64), ("hgrn_out", 16)):
        out += [(name, i, True) for i in range(n)]
    return out


class Queue:

    def __init__(self, sem):
        self.sem, self.count, self.items, self.seen = sem, 0, [], {}

    def put(self, fn, *waits):
        todo = []
        for m in waits:
            if m is None:
                continue
            sem, value = m
            if self.seen.get(id(sem), 0) < value:
                self.seen[id(sem)] = value
                todo.append((sem, value))
        self.count += 1
        self.items.append((todo, fn))
        return self.sem, self.count

    def emit(self, eng):
        for todo, fn in self.items:
            for sem, value in todo:
                eng.wait_ge(sem, value)
            fn(eng).then_inc(self.sem, 1)


def build(nc, a):
    with ExitStack() as ctx:
        def sb(name, shape, dt=F32):
            return ctx.enter_context(nc.sbuf_tensor(name, shape, dt))

        def sem(name):
            return ctx.enter_context(nc.semaphore(name))

        X = sb("X", [128, 8, T])
        HH = sb("HH", [128, 8, T], F32R)
        HL = sb("HL", [128, 8, T], F32R)
        RAW = sb("RAW", [128, NR, 1024])
        WH = sb("WH", [128, NS, 1024], F32R)
        WL = sb("WL", [128, NS, 1024], F32R)
        Z = sb("Z", [128, 32, T])
        ZH = sb("ZH", [128, NZ, T], F32R)
        ZL = sb("ZL", [128, NZ, T], F32R)
        VEC = sb("VEC", [128, V_N])
        CST = sb("CST", [128, C_D])
        MSK = sb("MSK", [128, 1024], U8)
        ONES = sb("ONES", [128, 128])
        MOD = sb("MOD", [128, 48])
        COL = sb("COL", [128, 96])
        RB = sb("RB", [128, T])
        DG = sb("DG", [128, T])
        TMP = sb("TMP", [128, 5, T])
        NW = sb("NW", [128, 6, 16])
        NWI = sb("NWI", [128, 2, 16], I32)
        PS = [ctx.enter_context(nc.psum_tensor(f"PS{i}", [128, T], F32)) for i in range(8)]

        s_raw = [sem(f"s_raw{i}") for i in range(NR)]
        s_vec, s_cst, s_x, s_pos, s_d, s_msk, s_out = (
            sem(n) for n in ("s_vec", "s_cst", "s_x", "s_pos", "s_d", "s_msk", "s_out"))
        PE, DV, AC, PO = (Queue(sem(n)) for n in ("s_pe", "s_dve", "s_act", "s_pool"))
        sp = []

        units = unit_list()
        split_of = [i for i, u in enumerate(units) if u[2]]
        freed = {}
        st = {"next": 0, "split": 0, "hi": 0, "unit": 0, "z": 0, "ada": 0}
        w_ready, w_used = {}, {}

        def load_unit(i):
            name, n, _ = units[i]
            m = freed.get(i - NR)
            sp.append(([m] if m else [], RAW[:, i % NR, :], a[name][n], s_raw[i % NR]))

        def landed(i):
            return s_raw[i % NR], 16 * (i // NR + 1)

        ACCS = [Z[:, 26 + 2 * i:28 + 2 * i, :].rearrange("p a b -> p (a b)") for i in range(2)]
        ada = {"acc": [None, None], "sum": None, "read": [None, None]}

        def sum_ada(i, n):
            j, k = divmod(n, 8)
            st["ada"] += 1
            src = RAW[:, i % NR, :]
            sc = COL[:, k:k + 1]
            b = j if j < 2 else 0
            ACC = ACCS[b]
            if k == 0:
                m = DV.put(lambda e: e.tensor_scalar(ACC, src, sc, None, ALU.mult),
                           landed(i), silu_c, ada["read"][b])
            else:
                m = DV.put(lambda e: e.scalar_tensor_tensor(out=ACC, in0=src, scalar=sc, in1=ACC,
                                                            op0=ALU.mult, op1=ALU.add),
                           landed(i), ada["acc"][b])
            ada["acc"][b] = m
            if k == 7:
                def mm(e):
                    for c in range(8):
                        r = e.matmul(PS[7][:, 16 + c:17 + c], ACC[:, 128 * c:128 * c + 128], ONES[:, 0:1],
                                     start=True, stop=True)
                    return r
                ada["read"][b] = PE.put(mm, m, ones, ada["sum"], small["free"])
                ada["sum"] = DV.put(
                    lambda e: e.tensor_tensor(MOD[:, 8 * j:8 * j + 8], PS[7][:, 16:24],
                                              VEC[:, V_BADA + 8 * j:V_BADA + 8 * j + 8], ALU.add),
                    ada["read"][b])
                small["free"] = ada["sum"]
                mod[j] = ada["sum"]
            return m

        def first_half():
            i = st["next"]
            if i >= len(units):
                return
            st["next"] += 1
            if units[i][2]:
                s = st["hi"]
                st["hi"] += 1
                hi = AC.put(lambda e: e.activation(WH[:, s % NS, :], RAW[:, i % NR, :], ACT.Copy),
                            landed(i), w_used.get(s - NS))
                halves.append((s, i, hi))
            else:
                freed[i] = sum_ada(i, units[i][1])
                if i + NR < len(units):
                    load_unit(i + NR)

        def second_half():
            s, i, hi = halves.pop(0)
            st["split"] += 1
            freed[i] = w_ready[s] = DV.put(
                lambda e: e.tensor_tensor(WL[:, s % NS, :], RAW[:, i % NR, :],
                                          WH[:, s % NS, :].bitcast(F32), ALU.subtract), hi)
            if i + NR < len(units):
                load_unit(i + NR)

        halves = []

        def prefetch(n):
            while st["hi"] < min(st["unit"] + n + 1, len(split_of)):
                first_half()
            while st["split"] < min(st["unit"] + n, len(split_of)):
                second_half()

        def unit():
            s = st["unit"]
            st["unit"] += 1
            prefetch(1)
            return s, s % NS

        mod, small = {}, {"free": None}
        bank_free = [None] * 8

        def three(e, out, wh, wl, xh, xl, first, last):
            e.matmul(out, wh, xh, start=first, stop=False)
            e.matmul(out, wh, xl, start=False, stop=False)
            return e.matmul(out, wl, xh, start=False, stop=last)

        def gemm4(banks, tokens, h_ready, evac):
            for q in range(4):
                s, slot = unit()
                wh = WH[:, slot, :].rearrange("p (k c) -> p k c", k=2)
                wl = WL[:, slot, :].rearrange("p (k c) -> p k c", k=2)
                for kk in range(2):
                    k = 2 * q + kk
                    for j in range(4):
                        cols = slice(128 * j, 128 * j + 128)

                        def mm(e, j=j, k=k, kk=kk, cols=cols, wh=wh, wl=wl):
                            if tokens:
                                return three(e, PS[banks[j]][:, :], HH[:, k, cols], HL[:, k, cols],
                                             wh[:, kk, :], wl[:, kk, :], k == 0, k == 7)
                            return three(e, PS[banks[j]][:, :], wh[:, kk, cols], wl[:, kk, cols],
                                         HH[:, k, :], HL[:, k, :], k == 0, k == 7)
                        m = PE.put(mm, w_ready[s], h_ready[k], bank_free[banks[j]] if k == 0 else None)
                        if k == 7:
                            evac(j, m)
                    if kk == 0:
                        prefetch(2)
                    yield
                w_used[s] = m

        def gemm1(bank, h_ready, evac, last=True):
            s, slot = unit()
            for k in range(8):
                cols = slice(128 * k, 128 * k + 128)
                m = PE.put(lambda e, k=k, cols=cols: three(
                    e, PS[bank][:, :], WH[:, slot, cols], WL[:, slot, cols], HH[:, k, :], HL[:, k, :],
                    k == 0, k == 7 and last), w_ready[s], h_ready[k], bank_free[bank] if k == 0 else None)
                if k == 3:
                    prefetch(2)
                if k == 7:
                    w_used[s] = m
                    evac(m)
                yield

        def run(main, *side):
            for n, _ in enumerate(main):
                if n % 2 == 0:
                    for g in side:
                        next(g, None)

        def split_hi(src, n, ready):
            return AC.put(lambda e: e.activation(ZH[:, n % NZ, :], src, ACT.Copy), ready, z_used.get(n - NZ))

        def split_lo(src, n, hi):
            return DV.put(lambda e: e.tensor_tensor(ZL[:, n % NZ, :], src, ZH[:, n % NZ, :].bitcast(F32),
                                                    ALU.subtract), hi)

        z_used = {}

        def gemm_out(nk, z_ready, evac, order=range(8), k0=0):
            base = st["z"] - k0
            st["z"] += nk - k0
            ready = {}
            for k in range(k0, k0 + 2):
                ready[k] = split_lo(Z[:, k, :], base + k, split_hi(Z[:, k, :], base + k, z_ready[k]))
            for k in range(k0, nk):
                s, slot = unit()
                if k + 2 < nk:
                    hi = split_hi(Z[:, k + 2, :], base + k + 2, z_ready[k + 2])
                z = (base + k) % NZ
                for n, f in enumerate(order if k == nk - 1 else range(8)):
                    if n == 4 and k + 2 < nk:
                        ready[k + 2] = split_lo(Z[:, k + 2, :], base + k + 2, hi)
                    if n == 6:
                        prefetch(2)
                    cols = slice(128 * f, 128 * f + 128)
                    m = PE.put(lambda e, f=f, k=k, cols=cols, z=z, slot=slot: three(
                        e, PS[f][:, :], WH[:, slot, cols], WL[:, slot, cols], ZH[:, z, :], ZL[:, z, :],
                        k == 0, k == nk - 1), w_ready[s], ready[k], bank_free[f] if k == 0 else None)
                    if k == nk - 1:
                        evac(f, m)
                w_used[s] = z_used[base + k] = m

        def column_sums(src, col, ready, first=True, last=True):
            def mm(e):
                for j in range(4):
                    r = e.matmul(PS[7][:, col + j:col + j + 1], src[:, 128 * j:128 * j + 128], ONES[:, 0:1],
                                 start=first and j == 0, stop=last, skip_group_check=True)
                return r
            return PE.put(mm, ones, ready, small["free"] if first else None, bank_free[7] if first else None)

        def rsqrt(n, scale, ready):
            x, y, t, xh = (NW[:, i, 0:n] for i in (4, 1, 2, 3))
            i0, i1 = NWI[:, 0, 0:n], NWI[:, 1, 0:n]
            m = DV.put(lambda e: e.tensor_scalar(x, PS[7][:, 0:n], scale, EPS, ALU.mult, ALU.add),
                       ready, nw["used"])
            small["free"] = m
            m2 = DV.put(lambda e: e.tensor_single_scalar(i0, x.bitcast(I32), 1, ALU.logical_shift_right), m)
            m1 = DV.put(lambda e: e.tensor_scalar(xh, x, -0.5, None, ALU.mult), m)
            m = m2
            m = DV.put(lambda e: e.tensor_scalar(i1, i0, -1.0, 1597463007.0, ALU.mult, ALU.add), m)
            cur = i1.bitcast(F32)
            for it in range(3):
                src = cur
                m = DV.put(lambda e, src=src: e.tensor_tensor(t, src, src, ALU.mult), m)
                m = DV.put(lambda e: e.tensor_tensor(t, t, xh, ALU.mult), m, m1)
                dst = y if it % 2 else NW[:, 0, 0:n]
                m = DV.put(lambda e, src=src, dst=dst: e.scalar_tensor_tensor(
                    out=dst, in0=t, scalar=1.5, in1=src, op0=ALU.add, op1=ALU.mult), m)
                cur = dst
            return m

        nw = {"used": None}

        def diagonal(c0, ready):
            for j in range(4):
                m = DV.put(lambda e, j=j: e.tensor_scalar(
                    DG[:, 128 * j:128 * j + 128], IDN, NW[:, 0, c0 + j:c0 + j + 1], None, ALU.mult),
                    ready, dg["used"])
            nw["used"] = m
            return m

        def spread(bank, ready):
            dg["used"] = PE.put(lambda e: e.matmul(PS[bank][:, :], ONES[:, :], DG[:, :], start=True,
                                                   stop=True), ready, ones, bank_free[bank])
            return dg["used"]

        dg = {"used": None}
        rb = {"used": None}

        def factors(ready, copy=True):
            m = spread(6, diagonal(0, rsqrt(4, 1.0 / 1024, ready)))
            if not copy:
                return m
            m = AC.put(lambda e: e.activation(RB[:, :], PS[6][:, :], ACT.Copy), m, rb["used"])
            bank_free[6] = m
            return m

        tmp_free = [None] * 5
        h_used = {"m": None}

        def make_h(gain, shift, x_ready, ready):
            out = []
            prefetch(2)
            his = {}
            for k in range(9):
                if k < 8:
                    t = TMP[:, k % 2, :]
                    m = DV.put(lambda e, k=k, t=t: e.scalar_tensor_tensor(
                        out=t, in0=X[:, k, :], scalar=gain[:, k:k + 1], in1=PS[6][:, :], op0=ALU.mult,
                        op1=ALU.mult), ready, x_ready[k], tmp_free[k % 2])
                    bank_free[6] = m
                    if shift is None:
                        his[k] = AC.put(lambda e, k=k, t=t: e.activation(HH[:, k, :], t, ACT.Copy),
                                        m, h_used["m"])
                    else:
                        his[k] = AC.put(lambda e, k=k, t=t: e.activation(
                            HH[:, k, :], t, ACT.Identity, bias=shift[:, k:k + 1]), m, h_used["m"])
                if k > 0:
                    j = k - 1
                    t = TMP[:, j % 2, :]
                    if shift is None:
                        m = DV.put(lambda e, j=j, t=t: e.tensor_tensor(
                            HL[:, j, :], t, HH[:, j, :].bitcast(F32), ALU.subtract), his[j])
                    else:
                        m = DV.put(lambda e, j=j, t=t: e.scalar_tensor_tensor(
                            out=HL[:, j, :], in0=t, scalar=shift[:, j:j + 1], in1=HH[:, j, :].bitcast(F32),
                            op0=ALU.add, op1=ALU.subtract), his[j])
                    tmp_free[j % 2] = m
                    out.append(m)
            return out

        def scaled(k, gain, ready):
            hi = AC.put(lambda e: e.activation(HH[:, k, :], X[:, k, :], ACT.Copy, scale=gain[:, k:k + 1]),
                        ready, h_used["m"])
            return DV.put(lambda e: e.scalar_tensor_tensor(
                out=HL[:, k, :], in0=X[:, k, :], scalar=gain[:, k:k + 1], in1=HH[:, k, :].bitcast(F32),
                op0=ALU.mult, op1=ALU.subtract), hi)

        LATE = (0, 1, 2, 3, 4, 5)

        def late_factors(x_ready, box):
            for k in range(8):
                m = square_acc(X[:, k, :], x_ready[k], k)
                if k in LATE:
                    yield
            m = rsqrt(4, 1.0 / 1024, m)
            box["c"] = DV.put(lambda e: e.tensor_copy(COL[:, 88:92], NW[:, 0, 0:4]), m, rb["used"])
            d = diagonal(0, m)
            yield
            m = spread(6, d)
            box["r"] = bank_free[6] = AC.put(lambda e: e.activation(RB[:, :], PS[6][:, :], ACT.Copy),
                                             m, rb["used"])
            yield

        IDN = CST[:, C_ID:C_ID + 128]

        sp.append(([], VEC[:, :], a["vec"], s_vec))
        sp.append(([], CST[:, :], a["cst"][:, 0:C_D], s_cst))
        POSI = Z[:, 31, :].bitcast(I32)
        vec, cst, x_in = (s_vec, 16), (s_cst, 16), (s_x, 16)
        for i in range(NR):
            load_unit(i)
        sp.append(([], X[:, :, :], a["x"].rearrange("(k p) t -> p k t", p=128), s_x))
        DMASK = Z[:, 22:26, :]

        def late_loads():
            sp.append(([], POSI, a["positions"].partition_broadcast(128), s_pos))
            sp.append(([], Z[:, 0:2, :].rearrange("p a b -> p (a b)"), a["msk"], s_msk))
            sp.append(([], DMASK, a["cst"][:, C_D:C_N].rearrange("p (h t) -> p h t", h=4), s_d))

        ones = DV.put(lambda e: e.memset(ONES[:, :], 1.0))
        m = AC.put(lambda e: e.activation(COL[:, 8:16], VEC[:, V_C:V_C + 8], ACT.Sigmoid), vec)
        silu_c = DV.put(lambda e: e.tensor_tensor(COL[:, 0:8], COL[:, 8:16], VEC[:, V_C:V_C + 8],
                                                  ALU.mult), m, ones)

        def square_acc(src, ready, k, group=8):
            q = k % group
            acc = SQ[:, (k // group) % 2, :]
            if q == 0:
                m = AC.put(lambda e: e.activation(acc, src, ACT.Square), ready, sq_free[(k // group) % 2])
            else:
                t = TMP[:, 2 + k % 2, :]
                m = AC.put(lambda e: e.activation(t, src, ACT.Square), ready, tmp_free[2 + k % 2])
                m = DV.put(lambda e: e.tensor_tensor(acc, acc, t, ALU.add), m, sq["acc"])
                tmp_free[2 + k % 2] = m
            sq["acc"] = m
            if q == group - 1:
                m = column_sums(acc, 0, m, first=k == q, last=k == 7)
                sq_free[(k // group) % 2] = m
            return m

        sq, sq_free = {"acc": None}, [None, None]
        SQ = sb("SQ", [128, 2, T])

        for n in range(16):
            first_half()
            if n in (3, 4, 5, 6):
                for k in (2 * n - 6, 2 * n - 5):
                    m = square_acc(X[:, k, :], x_in, k, 2)
            if n == 8:
                r1 = factors(m, copy=False)
                late_loads()

        COS, SIN = Z[:, 20, :], Z[:, 21, :]

        def angles():
            ANG, TN = Z[:, 30, :], TMP[:, 4, :]
            m = DV.put(lambda e: e.tensor_copy(TN, POSI), (s_pos, 16))
            m = DV.put(lambda e: e.tensor_scalar(ANG, TN, CST[:, C_FREQ:C_FREQ + 1], None, ALU.mult), m, cst)
            m = DV.put(lambda e: e.tensor_scalar(TN, ANG, float(np.float32(1 / (2 * np.pi))), 12582912.0,
                                                 ALU.mult, ALU.add), m)
            m = DV.put(lambda e: e.tensor_scalar(TN, TN, 12582912.0, None, ALU.subtract), m)
            for part in TWO_PI:
                m = DV.put(lambda e, part=part: e.scalar_tensor_tensor(
                    out=ANG, in0=TN, scalar=-part, in1=ANG, op0=ALU.mult, op1=ALU.add), m)
            msin = AC.put(lambda e: e.activation(SIN, ANG, ACT.Sin, scale=0.5), m)
            m = DV.put(lambda e: e.scalar_tensor_tensor(
                out=TN, in0=ANG, scalar=-1.0, in1=ANG, op0=ALU.mult, op1=ALU.max), m)
            m = AC.put(lambda e: e.activation(COS, TN, ACT.Sin, scale=-0.5, bias=CST[:, C_HPI:C_HPI + 1]), m)
            m1 = DV.put(lambda e: e.tensor_tensor(TN, SIN, SIN, ALU.mult), msin, m)
            m = DV.put(lambda e: e.scalar_tensor_tensor(out=SIN, in0=SIN, scalar=CST[:, C_SGN:C_SGN + 1],
                                                        in1=COS, op0=ALU.mult, op1=ALU.mult), m1)
            return DV.put(lambda e: e.tensor_scalar(COS, TN, -2.0, 1.0, ALU.mult, ALU.add), m)

        GA = COL[:, 16:24]
        m = DV.put(lambda e: e.scalar_tensor_tensor(
            out=GA, in0=MOD[:, 8:16], scalar=1.0, in1=VEC[:, V_GPRE1:V_GPRE1 + 8], op0=ALU.add,
            op1=ALU.mult), mod[1])
        m = DV.put(lambda e: e.tensor_copy(COL[:, 24:32], MOD[:, 0:8]), m, mod[0])
        h_ready = make_h(GA, COL[:, 24:32], [x_in] * 8, DV.put(
            lambda e: e.tensor_copy(COL[:, 32:33], COL[:, 16:17]), m, r1))


        z_ready = [None] * 32
        v_ready = [None] * 4
        VT = Z[:, 16:20, :]

        def evac_v(j, m):
            v_ready[j] = AC.put(lambda e: e.activation(VT[:, j, :], PS[j][:, :], ACT.Copy), m)
            bank_free[j] = v_ready[j]
        v_group = gemm4([0, 1, 2, 3], True, h_ready, evac_v)
        next(v_group)
        next(v_group)
        rot = angles()
        masks = DV.put(lambda e: e.tensor_copy(MSK[:, :], Z[:, 0:2, :].rearrange("p a b -> p (a b)")),
                       (s_msk, 16))
        run(v_group)

        def temp(i, fn, eng, *waits):
            m = eng.put(fn, tmp_free[i], *waits)
            return m

        qk_ready = [None] * 8

        def evac_rot(n, bank):
            def go(m):
                ps, b, out = PS[bank], TMP[:, n % 2, :], Z[:, 8 + n, :]
                DV.put(lambda e: e.tensor_tensor(b[0:64, :], ps[64:128, :], SIN[0:64, :], ALU.mult),
                       m, rot, tmp_free[n % 2])
                m1 = DV.put(lambda e: e.tensor_tensor(b[64:128, :], ps[0:64, :], SIN[64:128, :], ALU.mult), m)
                m2 = DV.put(lambda e: e.tensor_tensor(out, ps[:, :], COS, ALU.mult), m)
                bank_free[bank] = m2
                m = DV.put(lambda e: e.tensor_tensor(out, out, b, ALU.add), m1, m2)
                tmp_free[n % 2] = qk_ready[n] = m
            return go

        def evac_silu(dst, bank, done, owner=None):
            def go(m):
                m = AC.put(lambda e: e.activation(dst, PS[bank][:, :], ACT.Sigmoid), m,
                           owner and owner.free)
                m = DV.put(lambda e: e.tensor_tensor(dst, dst, PS[bank][:, :], ALU.mult), m)
                bank_free[bank] = m
                done(m)
            return go

        ring = [4, 5, 6]
        nb = 0
        for n in range(8):
            run(gemm1(ring[nb % 3], h_ready, evac_rot(n, ring[nb % 3])))
            nb += 1
        sg_ready = [None] * 4
        for n in range(4):
            def done(m, n=n):
                sg_ready[n] = m
            run(gemm1(ring[nb % 3], h_ready, evac_silu(Z[:, 4 + n, :], ring[nb % 3], done)))
            nb += 1

        def retention(h):
            A = Z[:, 28:31, :].rearrange("p a b -> p (a b)")
            off = [0, 512, 896, 1152]
            ready = []
            for i in range(4):
                n = T - 128 * i
                bank = i % 2
                m = PE.put(lambda e, i=i, n=n, bank=bank: e.matmul(
                    PS[bank][:, 0:n], Z[:, 12 + h, 128 * i:128 * i + 128], Z[:, 8 + h, 128 * i:T],
                    start=True, stop=True), qk_ready[h], qk_ready[4 + h], bank_free[bank])
                m = DV.put(lambda e, i=i, n=n, bank=bank: e.tensor_tensor(
                    A[:, off[i]:off[i] + n], PS[bank][:, 0:n], DMASK[:, h, 0:n], ALU.mult),
                    m, (s_d, 16), ret["a"], rot)
                bank_free[bank] = m
                ready.append(m)
                yield
            ob = 2 + h % 2
            for i in range(4):
                n = T - 128 * i
                m = PE.put(lambda e, i=i, n=n: e.matmul(
                    PS[ob][:, 128 * i:T], VT[:, i, 128 * h:128 * h + 128], A[:, off[i]:off[i] + n],
                    start=i == 0, stop=i == 3), ready[i], v_ready[i], bank_free[ob])
                yield
            ret["a"] = m
            t = TMP[:, 2 + h % 2, :]
            m1 = AC.put(lambda e: e.activation(t, PS[ob][:, :], ACT.Square), m, tmp_free[2 + h % 2])
            m2 = DV.put(lambda e: e.tensor_tensor(Z[:, 4 + h, :], PS[ob][:, :], Z[:, 4 + h, :], ALU.mult),
                        m, sg_ready[h], m1)
            bank_free[ob] = m2
            yield
            ret["sum"] = column_sums(t, 4 * h, m1, first=True)
            tmp_free[2 + h % 2] = ret["sum"]
            ret["z"][h] = m2
            yield

        ret = {"a": None, "sum": None, "z": [None] * 4}

        def ret_norm():
            m = rsqrt(16, 1.0 / 128, ret["sum"])
            for h in range(4):
                bank = h % 2
                d = diagonal(4 * h, m)
                yield
                m1 = spread(bank, d)
                z_ready[4 + h] = DV.put(lambda e, h=h, bank=bank: e.tensor_tensor(
                    Z[:, 4 + h, :], Z[:, 4 + h, :], PS[bank][:, :], ALU.mult), m1, ret["z"][h])
                bank_free[bank] = z_ready[4 + h]
                yield

        def chain(*gens):
            for g in gens:
                yield from g

        side = chain(*(retention(h) for h in range(4)), ret_norm())

        conv = {}

        def evac_x(i, bank):
            def go(m):
                conv["x"] = AC.put(lambda e: e.activation(TMP[:, 0, :], PS[bank][:, :], ACT.Copy),
                                   m, tmp_free[0])
                bank_free[bank] = conv["x"]
            return go

        def evac_c(i, bank):
            def go(m):
                u = TMP[:, 1, :]
                y = Z[:, i, :]
                w = [VEC[:, V_CONV + 4 * j + i:V_CONV + 4 * j + i + 1] for j in range(3)]
                m = DV.put(lambda e: e.tensor_tensor(u, TMP[:, 0, :], PS[bank][:, :], ALU.mult),
                           m, conv["x"], tmp_free[1])
                bank_free[bank] = tmp_free[0] = m
                m = DV.put(lambda e: e.tensor_scalar(y, u, w[2], None, ALU.mult), m)
                for j in (1, 2):
                    m = DV.put(lambda e, j=j: e.scalar_tensor_tensor(
                        out=y[:, j:T], in0=u[:, 0:T - j], scalar=w[2 - j], in1=y[:, j:T],
                        op0=ALU.mult, op1=ALU.add), m)
                tmp_free[1] = conv["y"] = m
            return go

        def evac_b(i, bank):
            def go(m):
                z_ready[i] = DV.put(lambda e: e.tensor_tensor(Z[:, i, :], Z[:, i, :], PS[bank][:, :],
                                                              ALU.mult), m, conv["y"])
                bank_free[bank] = z_ready[i]
            return go

        for i in range(4):
            for ev in (evac_x, evac_c, evac_b):
                run(gemm1(ring[nb % 3], h_ready, ev(i, ring[nb % 3])), side)
                nb += 1
        for _ in side:
            pass
        h_used["m"] = (PE.sem, PE.count)
        while st["ada"] < 48:
            first_half()

        def gains(dst, j, g, one):
            return DV.put(lambda e: e.scalar_tensor_tensor(
                out=COL[:, dst:dst + 8], in0=MOD[:, 8 * j:8 * j + 8], scalar=1.0 if one else 0.0,
                in1=VEC[:, g:g + 8], op0=ALU.add, op1=ALU.mult), mod[j])

        def residual(nk, z_ready, gate, gate_ready, x_ready, gain=None):
            y, sums = {}, []

            def evac(f, m):
                if f >= 6:
                    y[f] = (Z[:, f, :], AC.put(lambda e: e.activation(Z[:, f, :], PS[f][:, :], ACT.Copy), m))
                    bank_free[f] = y[f][1]
                else:
                    y[f] = (PS[f][:, :], m)
                sums.append(square_acc(y[f][0], y[f][1], len(sums)))
            gemm_out(nk, z_ready, evac, [6, 7, 0, 1, 2, 3, 4, 5])
            r = factors(sums[-1])
            prefetch(2)
            out, h = [], []
            for n, f in enumerate([6, 7, 0, 1, 2, 3, 4, 5] if gain is None else range(8)):
                t = TMP[:, n % 2, :]
                m = DV.put(lambda e, f=f, t=t: e.scalar_tensor_tensor(
                    out=t, in0=y[f][0], scalar=gate[:, f:f + 1], in1=RB[:, :], op0=ALU.mult,
                    op1=ALU.mult), r, y[f][1], gate_ready, tmp_free[n % 2])
                if f < 6:
                    bank_free[f] = m
                m = DV.put(lambda e, f=f, t=t: e.tensor_tensor(X[:, f, :], X[:, f, :], t, ALU.add),
                           m, x_ready[f])
                tmp_free[n % 2] = m
                out.append((f, m))
                if gain is None:
                    m = square_acc(X[:, f, :], m, n, 1)
                else:
                    h.append((f, scaled(f, gain, m)))
            rb["used"] = out[-1][1]
            return [m for _, m in sorted(out)], [m for _, m in h] if h else factors(m, copy=False)

        g1 = gains(32, 2, V_GPOST1, False)
        g2 = gains(40, 4, V_GPRE2, True)
        g3 = gains(48, 5, V_GPOST2, False)
        b2 = DV.put(lambda e: e.tensor_copy(COL[:, 56:64], MOD[:, 24:32]), mod[3])
        x_ready, r = residual(8, z_ready, COL[:, 32:40], g1, [x_in] * 8)

        m = DV.put(lambda e: e.tensor_copy(COL[:, 64:65], COL[:, 40:41]), g2, g3, b2)
        h_ready = make_h(COL[:, 40:48], COL[:, 56:64], x_ready, r)

        def evac_relu(f, bank):
            def go(m):
                t = TMP[:, f % 2, :]
                m = AC.put(lambda e: e.activation(t, PS[bank][:, :], ACT.Relu), m, tmp_free[f % 2])
                bank_free[bank] = m
                z_ready[f] = tmp_free[f % 2] = DV.put(
                    lambda e: e.tensor_tensor(Z[:, f, :], t, t, ALU.mult), m)
            return go
        run(gemm4([0, 1, 2, 3], False, h_ready, lambda j, m: evac_relu(j, j)(m)))
        for f in range(4, 32):
            bank = f % 8
            run(gemm1(bank, h_ready, evac_relu(f, bank)))
        h_used["m"] = (PE.sem, PE.count)
        x_ready, h_ready = residual(32, z_ready, COL[:, 48:56], g3, x_ready, VEC[:, V_NG0:V_NG0 + 8])

        r = h_ready[-1]
        norm = {}

        def with_factors(products, x_ready, evacs):
            late = late_factors(x_ready, norm)
            for _ in products:
                next(late, None)
            for _ in late:
                pass
            for go in evacs:
                go()
        PADW = 16 + T
        flat = Z[:, 20:32, :].rearrange("p a b -> p (a b)")
        VP, S1, S2, PP = (flat[:, PADW * i:PADW * (i + 1)] for i in range(4))
        pads = DV.put(lambda e: e.memset(flat[:, 0:4 * PADW], 0.0), r, (PE.sem, PE.count))
        pool = {"free": pads, "p": {}, "g": {}}

        def window(g, j, bank):
            def go(m):
                w = 2 << g
                m = DV.put(lambda e: e.tensor_tensor(VP[:, 16:PADW], PS[bank][:, :], RB[:, :], ALU.mult),
                           m, pool["free"], norm["r"])
                bank_free[bank] = m
                src, dst = VP, S1
                for lev in range(g + 1):
                    sh = 1 << lev
                    m = DV.put(lambda e, src=src, dst=dst, sh=sh: e.tensor_tensor(
                        dst[:, 16:PADW], src[:, 16:PADW], src[:, 16 - sh:PADW - sh], ALU.add), m)
                    src, dst = dst, (S2 if dst is S1 else S1)
                p = PP[:, 0:T]
                m1 = DV.put(lambda e: e.scalar_tensor_tensor(
                    out=p[:, 16:T], in0=src[:, 32:PADW], scalar=1.0 / w, in1=VP[:, 32:PADW],
                    op0=ALU.mult, op1=ALU.subtract), m)
                m2 = DV.put(lambda e: e.tensor_tensor(
                    p[:, 0:16], src[:, 16:32], CST[:, C_CNT + 16 * g:C_CNT + 16 * g + 16], ALU.mult), m)
                m = DV.put(lambda e: e.tensor_tensor(p[:, 0:16], p[:, 0:16], VP[:, 16:32], ALU.subtract), m2)
                hi = AC.put(lambda e: e.activation(PHI(j), p, ACT.Copy), m, m1, grp["used"])
                m = DV.put(lambda e: e.tensor_tensor(PLO(j), p, PHI(j).bitcast(F32), ALU.subtract), hi)
                pool["free"] = m
                pool["p"][j] = m
            return go

        def evac_silu_scaled(dst, bank, done, owner=None, later=None):
            def go(m):
                t = TMP[:, 4, :]
                m = DV.put(lambda e: e.tensor_tensor(t, PS[bank][:, :], RB[:, :], ALU.mult),
                           m, norm["r"], tmp_free[4])
                bank_free[bank] = m
                m1 = AC.put(lambda e: e.activation(dst, t, ACT.Sigmoid), m, owner and owner.free)

                def last():
                    m = DV.put(lambda e: e.tensor_tensor(dst, dst, t, ALU.mult), m1)
                    tmp_free[4] = rb["used"] = m
                    done(m)
                if later is None:
                    last()
                else:
                    later.append(last)
            return go

        scope = ctx.enter_context(ExitStack())
        PSP = scope.enter_context(nc.sbuf_tensor("PSP", [128, 4, T], F32R))

        def PHI(j):
            return PSP[:, j, :]

        def PLO(j):
            return (ZH if j < 3 else ZL)[:, j % 3, :]
        grp = {"used": (PE.sem, PE.count)}
        for g in range(4):
            if g == 0:
                evacs = []
                first = gemm4([0, 1, 2, 3], False, h_ready,
                              lambda j, m: evacs.append(lambda: window(0, j, j)(m)))
            else:
                for j in range(4):
                    run(gemm1(j, h_ready, window(g, j, j)))
            for j in range(4):
                def done(m, j=j):
                    pool["g"][j] = m
                go = evac_silu_scaled(Z[:, 16 + j, :], 4 + j, done)
                if g == 0 and j == 0:
                    with_factors(chain(first, gemm1(4, h_ready, lambda m, go=go: evacs.append(
                        lambda: go(m)))), x_ready, evacs)
                else:
                    run(gemm1(4 + j, h_ready, go))
            for q in range(2):
                s, slot = unit()
                wh = WH[:, slot, :].rearrange("p (k c) -> p k c", k=4)
                wl = WL[:, slot, :].rearrange("p (k c) -> p k c", k=4)
                for i in range(2):
                    f = 2 * q + i
                    bank = f
                    cols = slice(128 * i, 128 * i + 128)
                    for k in range(4):
                        m = PE.put(lambda e, k=k, bank=bank, cols=cols, wh=wh, wl=wl: three(
                            e, PS[bank][:, :], wh[:, k, cols], wl[:, k, cols], PHI(k), PLO(k),
                            k == 0, k == 3), w_ready[s], pool["p"][k], bank_free[bank] if k == 0 else None)
                    zt = 4 * g + f
                    z_ready[zt] = DV.put(lambda e, zt=zt, f=f, bank=bank: e.scalar_tensor_tensor(
                        out=Z[:, zt, :], in0=PS[bank][:, :], scalar=VEC[:, V_PS + zt:V_PS + zt + 1],
                        in1=Z[:, 16 + f, :], op0=ALU.mult, op1=ALU.mult), m, pool["g"][f])
                    bank_free[bank] = z_ready[zt]
                w_used[s] = m
            grp["used"] = m
        h_used["m"] = (PE.sem, PE.count)

        def add_out(nk, x_ready, gain, k0=0):
            out, h, sums = {}, [], []

            def evac(f, m):
                m = DV.put(lambda e: e.tensor_tensor(X[:, f, :], X[:, f, :], PS[f][:, :], ALU.add),
                           m, x_ready[f])
                bank_free[f] = m
                out[f] = m
                if gain is None:
                    sums.append(square_acc(X[:, f, :], m, len(sums), 2))
                else:
                    h.append(scaled(f, gain, m))
            gemm_out(nk, z_ready, evac, range(8) if gain is not None else [7, 6, 0, 1, 2, 3, 4, 5], k0)
            return out, h if h else factors(sums[-1])

        for i in range(3):
            z_used[st["z"] - 1 - i] = grp["used"]
        x_ready, h_ready = add_out(16, x_ready, VEC[:, V_NG1:V_NG1 + 8])

        L0, L1 = VEC[:, V_LB:V_LB + 16], VEC[:, V_LB + 16:V_LB + 32]
        E0, E1, MX = NW[:, 4, :], NW[:, 5, :], NW[:, 3, :]
        LBC, OMC = COL[:, 0:16], COL[:, 16:32]
        last = (DV.sem, DV.count)
        m = DV.put(lambda e: e.tensor_tensor(MX, L0, L1, ALU.max), last)
        m1 = DV.put(lambda e: e.tensor_tensor(E0, L0, MX, ALU.subtract), m)
        m2 = DV.put(lambda e: e.tensor_tensor(E1, L1, MX, ALU.subtract), m)
        m1 = AC.put(lambda e: e.activation(E0, E0, ACT.Exp), m1, m2)
        m2 = AC.put(lambda e: e.activation(E1, E1, ACT.Exp), m2)
        m = DV.put(lambda e: e.tensor_tensor(MX, E0, E1, ALU.add), m1, m2)
        m = DV.put(lambda e: e.reciprocal(MX, MX), m)
        m1 = DV.put(lambda e: e.tensor_tensor(E0, E0, MX, ALU.mult), m)
        m2 = DV.put(lambda e: e.tensor_tensor(E1, E1, MX, ALU.mult), m)
        m = DV.put(lambda e: e.tensor_tensor(MX, E0, E1, ALU.add), m1, m2)
        m = DV.put(lambda e: e.tensor_tensor(LBC, MX, E0, ALU.subtract), m)
        m = DV.put(lambda e: e.tensor_scalar(OMC, LBC, -1.0, 1.0, ALU.mult, ALU.add), m)
        lb_ready = DV.put(lambda e: e.tensor_scalar(LBC, LBC, 2.0 ** -24, None, ALU.max), m)
        nw["used"] = lb_ready

        norm.clear()
        hv_ready = [None] * 16
        z_last = (PE.sem, PE.count)
        for g in range(4):
            banks = [0, 1, 2, 3] if g % 2 == 0 else [4, 5, 6, 7]

            def evac_hv(j, m, g=g, banks=banks):
                m = AC.put(lambda e: e.activation(
                    Z[:, 4 * g:4 * g + 4, 128 * j:128 * j + 128],
                    PS[banks[j]][:, :].rearrange("p (h v) -> p h v", h=4), ACT.Copy,
                    scale=COL[:, 88 + j:89 + j]), m, z_last, norm["c"])
                bank_free[banks[j]] = m
                for h in range(4):
                    hv_ready[4 * g + h] = m
            if g == 0:
                evacs = []
                with_factors(gemm4(banks, True, h_ready,
                                   lambda j, m: evacs.append(lambda: evac_hv(j, m))), x_ready, evacs)
            else:
                run(gemm4(banks, True, h_ready, evac_hv))

        hflat = Z[:, 16:32, :].rearrange("p a b -> p (a b)")

        class Head:
            def __init__(self, b):
                base = 4096 * b
                self.A = hflat[:, base:base + 2048]
                self.wide = hflat[:, base:base + 2560]
                self.tot = hflat[:, base + 512:base + 640]
                self.q, self.f, self.k, self.sg = (
                    hflat[:, base + 2048 + T * i:base + 2560 + T * i] for i in range(4))
                self.free = DV.put(lambda e: e.memset(self.A, 0.0), z_last)
        heads = [Head(0), Head(1)]
        scope.close()
        QP0, QP1, W, IW = (sb(n, [128, T]) for n in ("QP0", "QP1", "W", "IW"))
        QP = [QP0, QP1]
        w3 = DV.put(lambda e: e.memset(W[:, :], 1.0), z_last)
        LVB, OB, RBK = [3, 4], 5, 6
        hz = [None] * 16
        lv = {"n": 0}
        w_free = {"m": w3}

        def parts(x, L):
            v = x.rearrange("p (n a l) -> p n a l", a=2, l=L)
            return v[:, :, 0, :], v[:, :, 1, :]

        def project(h):
            b = heads[h % 2]
            qp = QP[h % 2][:, :]
            col = slice(h, h + 1)

            def ev_f(m):
                m = DV.put(lambda e: e.tensor_tensor(b.f, PS[0][:, :], RB[:, :], ALU.mult),
                           m, b.free, norm["r"])
                bank_free[0] = m
                m2 = AC.put(lambda e: e.activation(b.k, b.f, ACT.Sigmoid, scale=-1.0), m, b.free)
                m1 = AC.put(lambda e: e.activation(b.f, b.f, ACT.Sigmoid), m, m2)
                b.sigmoids = m1, m2
                prep.append(prepare(h))

            def ev_q(m):
                b.q_ready = DV.put(lambda e: e.tensor_tensor(b.q, PS[1][:, :], RB[:, :], ALU.mult),
                                   m, b.free, norm["r"])
                bank_free[1] = b.q_ready

            def done(m):
                b.sg_ready = m
            yield from gemm1(0, h_ready, ev_f)
            yield from gemm1(1, h_ready, ev_q)
            yield from gemm1(2, h_ready, evac_silu_scaled(b.sg, 2, done, b, gates))

        def prepare(h):
            b = heads[h % 2]
            qp = QP[h % 2][:, :]
            col = slice(h, h + 1)
            if True:
                m1, m2 = b.sigmoids
                m = DV.put(lambda e: e.tensor_scalar(b.f, b.f, OMC[:, col], LBC[:, col], ALU.mult,
                                                     ALU.add), m1, lb_ready)
                b.k_ready = DV.put(lambda e: e.tensor_scalar(b.k, b.k, OMC[:, col], None, ALU.mult), m2)
                yield
                w8 = W[:, :].rearrange("p (n l) -> p n l", l=8)
                f8 = b.f.rearrange("p (n l) -> p n l", l=8)
                m = DV.put(lambda e: e.tensor_copy(w8[:, :, 2:5:2], f8[:, :, 3:5]), m, w_free["m"])
                yield
                m = DV.put(lambda e: e.tensor_tensor(w8[:, :, 1:6:4], w8[:, :, 2:5:2], f8[:, :, 2:6:3],
                                                     ALU.mult), m)
                m = DV.put(lambda e: e.tensor_tensor(w8[:, :, 0:7:6], w8[:, :, 1:6:4], f8[:, :, 1:7:5],
                                                     ALU.mult), m)
                yield
                m1 = DV.put(lambda e: e.tensor_tensor(w8[:, :, 7], w8[:, :, 6], f8[:, :, 7], ALU.mult), m)
                b.tl_ready = DV.put(lambda e: e.tensor_tensor(b.tot[:, 64:128], w8[:, :, 0], f8[:, :, 0],
                                                              ALU.mult), m, b.free)
                for i in range(4):
                    yield
                    c = slice(128 * i, 128 * i + 128)
                    b.w_ready = DV.put(lambda e, c=c: e.reciprocal(IW[:, c], W[:, c]), m1, w_free["m"])
                yield
                (q0, q1), (p0, p1), (w0, w1), (i0, i1), (k0, k1), (f0, f1) = (
                    parts(x, 4) for x in (b.q, qp, W[:, :], IW[:, :], b.k, b.f))
                DV.put(lambda e: e.tensor_tensor(f0, k0, w0, ALU.mult), b.w_ready, b.k_ready, b.tl_ready)
                yield
                kt = DV.put(lambda e: e.tensor_tensor(f1, k1, i1, ALU.mult), b.w_ready)
                yield
                DV.put(lambda e: e.tensor_tensor(p0, q0, i0, ALU.mult), b.w_ready, b.q_ready, b.free)
                b.t_ready = DV.put(lambda e: e.tensor_tensor(p1, q1, w1, ALU.mult), b.w_ready)
                w8 = W[:, :].rearrange("p (n l) -> p n l", l=8)
                v8 = [x.rearrange("p (n l) -> p n l", l=8) for x in (b.q, qp, b.k, b.f)]
                tl = b.tot[:, 64:128].rearrange("p (n o) -> p n o", o=1)
                yield
                m1 = DV.put(lambda e: e.tensor_tensor(
                    v8[0], v8[1], tl.broadcast_to([128, 64, 8]), ALU.mult), b.t_ready)
                yield
                m2 = DV.put(lambda e: e.tensor_tensor(
                    v8[2], v8[3], w8[:, :, 7:8].broadcast_to([128, 64, 8]), ALU.mult), kt)
                m3 = DV.put(lambda e: e.tensor_tensor(b.tot[:, 0:64], w8[:, :, 7], b.tot[:, 64:128],
                                                      ALU.mult), b.tl_ready, m1)
                w_free["m"] = m3
                b.q8_ready, b.k8_ready, b.tot_ready = m1, m2, m3

        def mixing(h):
            b = heads[h % 2]
            qp = QP[h % 2]
            diag = b.wide.rearrange("p (i t) -> p i t", i=4)

            def bank_of_level():
                lv["n"] += 1
                return LVB[lv["n"] % 2]
            bank = bank_of_level()
            ps = PS[bank]

            def mm(e, ps=ps):
                for i in range(4):
                    c = slice(128 * i, 128 * i + 128)
                    r = e.matmul(ps[:, c], b.f[:, c], qp[:, c], start=True, stop=True)
                return r
            m = PE.put(mm, b.t_ready, bank_free[bank])
            a_ready = DV.put(lambda e, ps=ps: e.copy_predicated(
                diag[:, :, 0:128], MSK[:, 0:512].rearrange("p (i t) -> p i t", i=4),
                ps[:, :].rearrange("p (i t) -> p i t", i=4)), m, masks)
            bank_free[bank] = a_ready
            q_ready, k_ready, t_ready = b.q8_ready, b.k8_ready, b.tot_ready
            tot, at = b.tot[:, 0:64], 64
            yield
            for L in (8, 16, 32, 64, 128, 256):
                bank = bank_of_level()
                ps = PS[bank]
                k0, q1 = parts(b.k, L)[0], parts(b.q, L)[1]
                if L <= 32:
                    def mm(e, L=L, ps=ps):
                        for i in range(4):
                            c = slice(128 * i, 128 * i + 128)
                            o = ps[:, 64 * i:64 * i + 64].rearrange("p (n l) -> p n l", l=L)
                            r = e.matmul(o, b.k[:, c], parts(b.q[:, c], L)[1], start=True, stop=True)
                        return r
                elif L == 64:
                    def mm(e, ps=ps, k0=k0, q1=q1):
                        for i in range(4):
                            r = e.matmul(ps[0:64, 64 * i:64 * i + 64], k0[:, i, :], q1[:, i, :],
                                         start=True, stop=True)
                        return r
                elif L == 128:
                    def mm(e, ps=ps, k0=k0, q1=q1):
                        for i in range(2):
                            r = e.matmul(ps[:, 128 * i:128 * i + 128], k0[:, i, :], q1[:, i, :],
                                         start=True, stop=True)
                        return r
                else:
                    def mm(e, ps=ps):
                        for i in range(2):
                            r = e.matmul(ps[:, 256 * i:256 * i + 256], b.k[:, 128 * i:128 * i + 128],
                                         b.q[:, 256:512], start=True, stop=True)
                        return r
                used = PE.put(mm, q_ready, k_ready, bank_free[bank])
                if L < 256:
                    n = T // (2 * L)
                    tv = tot.rearrange("p (n a) -> p n a", a=2)
                    q_ready = DV.put(lambda e, q1=q1, tv=tv, n=n, L=L: e.tensor_tensor(
                        q1, q1, tv[:, :, 0:1].broadcast_to([128, n, L]), ALU.mult), used, t_ready, q_ready)
                    k_ready = DV.put(lambda e, k0=k0, tv=tv, n=n, L=L: e.tensor_tensor(
                        k0, k0, tv[:, :, 1:2].broadcast_to([128, n, L]), ALU.mult), used, t_ready, k_ready)
                    if L < 128:
                        nt = b.tot[:, at:at + n]
                        at += n
                        t_ready = DV.put(lambda e, nt=nt, tv=tv: e.tensor_tensor(
                            nt, tv[:, :, 0], tv[:, :, 1], ALU.mult), t_ready)
                        tot = nt
                if L <= 16:
                    ad = diag[:, :, 0:128].rearrange("p i (n a l) -> p i n a l", a=2, l=L)[:, :, :, 1, :]
                    o = 512 + 256 * (L // 16)
                    a_ready = DV.put(lambda e, ad=ad, ps=ps, o=o, L=L: e.copy_predicated(
                        ad, MSK[:, o:o + 256].rearrange("p (i n l) -> p i n l", i=4, l=L),
                        ps[:, 0:256].rearrange("p (i n l) -> p i n l", i=4, l=L)), used, a_ready)
                    m = a_ready
                elif L == 32:
                    for i in range(2):
                        s0 = 64 * i
                        m = AC.put(lambda e, i=i, s0=s0, ps=ps: e.activation(
                            diag[s0:s0 + 32, :, s0 + 32:s0 + 64],
                            ps[s0:s0 + 32, 0:256].rearrange("p (i t) -> p i t", i=4)[:, :, 32 * i:32 * i + 32],
                            ACT.Copy), used, a_ready)
                elif L == 64:
                    m = AC.put(lambda e, ps=ps: e.activation(
                        diag[0:64, :, 64:128], ps[0:64, 0:256].rearrange("p (i t) -> p i t", i=4),
                        ACT.Copy), used, a_ready)
                elif L == 128:
                    m = AC.put(lambda e, ps=ps: e.activation(
                        b.A[:, 128:1536].rearrange("p (x t) -> p x t", t=128)[:, 0:11:10, :],
                        ps[:, 0:256].rearrange("p (x t) -> p x t", t=128), ACT.Copy), used)
                else:
                    m = AC.put(lambda e, ps=ps: e.activation(
                        b.A[:, 0:1024].rearrange("p (x t) -> p x t", x=2)[:, :, 256:512],
                        ps[:, :].rearrange("p (x t) -> p x t", x=2), ACT.Copy), used)
                bank_free[bank] = m
                yield

            def pv(e):
                o, v = PS[OB], Z[:, h, :]
                for i in range(4):
                    r = e.matmul(o[:, 128 * i:T], v[:, 128 * i:128 * i + 128],
                                 b.A[:, 640 * i:512 * i + 512], start=i == 0, stop=i == 3)
                return r
            m = PE.put(pv, m, hv_ready[h], bank_free[OB])
            t = TMP[:, 2 + h % 2, :]
            m1 = AC.put(lambda e: e.activation(t, PS[OB][:, :], ACT.Square), m, tmp_free[2 + h % 2])
            hz[h] = DV.put(lambda e: e.scalar_tensor_tensor(
                out=Z[:, h, :], in0=PS[OB][:, :], scalar=VEC[:, V_HG + h:V_HG + h + 1], in1=b.sg,
                op0=ALU.mult, op1=ALU.mult), m, b.sg_ready, m1)
            bank_free[OB] = b.free = hz[h]
            yield
            m = column_sums(t, 4 * (h % 4), m1)
            tmp_free[2 + h % 2] = m
            if h % 4 == 3:
                m = rsqrt(16, 1.0 / 128, m)
                norms.append(norm4(h - 3, m))
            yield

        def norm4(h, m):
            for i in range(4):
                d = diagonal(4 * i, m)
                yield
                m1 = spread(RBK, d)
                z_ready[h + i] = DV.put(lambda e, i=i: e.tensor_tensor(
                    Z[:, h + i, :], Z[:, h + i, :], PS[RBK][:, :], ALU.mult), m1, hz[h + i])
                bank_free[RBK] = z_ready[h + i]
                yield

        norms, prep, gates, parts_z = [], [], [], [None] * 8
        SIDE = (1, 3, 5, 8, 11, 14, 17, 19, 21, 23)

        def split_z(k):
            hi = AC.put(lambda e: e.activation(HH[:, k, :], Z[:, k, :], ACT.Copy), z_ready[k], h_free[k])
            parts_z[k] = DV.put(lambda e: e.tensor_tensor(
                HL[:, k, :], Z[:, k, :], HH[:, k, :].bitcast(F32), ALU.subtract), hi)

        def out_columns(bank):
            return gemm1(bank, parts_z, lambda m: None, False)
        h_free = {}
        turn, side, ready = iter(()), iter(()), iter(())
        for h in range(17):
            for n, _ in enumerate(project(h) if h < 16 else chain(*(out_columns(f) for f in range(3)))):
                if h == 15 and n >= 16:
                    h_free[n - 16] = (PE.sem, PE.count)
                    if n >= 18:
                        split_z(n - 18)
                if n == 10 and prep:
                    ready = prep.pop()
                if n >= 10 or h:
                    next(ready, None)
                if n == 3 and gates:
                    gates.pop()()
                if n in SIDE:
                    next(side, None)
                    next(turn, None)
                if n == 0 and h:
                    side = mixing(h - 1)
                    turn = norms.pop() if norms else turn
                    if h == 16:
                        split_z(6)
                        split_z(7)
            for _ in ready:
                pass
            for _ in side:
                pass
        turn = norms.pop()
        for f in range(3, 6):
            for n, _ in enumerate(out_columns(f)):
                if n % 2:
                    next(turn, None)
        for _ in turn:
            pass
        for f in (6, 7):
            run(out_columns(f))
        x_ready, r = add_out(16, x_ready, None, 8)
        for f in range(8):
            m = DV.put(lambda e, f=f: e.scalar_tensor_tensor(
                out=Z[:, 16 + f, :], in0=X[:, f, :], scalar=VEC[:, V_FG + f:V_FG + f + 1], in1=RB[:, :],
                op0=ALU.mult, op1=ALU.mult), r, x_ready[f])
            sp.append(([m], a["out"][128 * f:128 * f + 128, :], Z[:, 16 + f, :], s_out))

        block = ctx.enter_context(nc.Block())

        @block.sync
        def _(e):
            for waits, dst, src, s in sp:
                for w in waits:
                    e.wait_ge(*w)
                e.dma_start(dst, src).then_inc(s, 16)
            e.wait_ge(s_out, 16 * 8)

        @block.tensor
        def _(e):
            PE.emit(e)

        @block.vector
        def _(e):
            DV.emit(e)

        @block.scalar
        def _(e):
            AC.emit(e)


def two_pi():
    rest, out = 2 * np.pi, []
    for _ in range(3):
        e = np.floor(np.log2(rest)) - 7
        part = np.floor(rest / 2.0 ** e) * 2.0 ** e
        out.append(float(part))
        rest -= part
    return out + [float(np.float32(rest))]


TWO_PI = two_pi()


def constants():
    c = np.zeros((128, C_N), np.float32)
    c[:, C_ID:C_ID + 128] = np.eye(128)
    half = np.arange(64, dtype=np.float32) / np.float32(64)
    c[:, C_FREQ] = np.tile((10000.0 ** -half.astype(np.float64)).astype(np.float32), 2)
    c[0:64, C_SGN], c[64:128, C_SGN] = -2.0, 2.0
    c[:, C_HPI] = np.pi / 2
    for g in range(4):
        c[:, C_CNT + 16 * g:C_CNT + 16 * g + 16] = 1.0 / np.minimum(np.arange(16) + 1.0, 2 << g)
    m, t = np.arange(128)[:, None], np.arange(T)[None, :]
    same = m // 64 == t // 64
    for h in range(4):
        gamma = 1.0 - 2.0 ** (-5.0 - h)
        d = np.where(same, gamma ** np.abs(t - m), np.where(t > m, gamma ** np.maximum(t - m, 0), 0.0))
        c[:, C_D + T * h:C_D + T * h + T] = d * 128.0 ** -0.5
    s, t = np.arange(128)[:, None], np.arange(128)[None, :]
    base = np.tile((s // 8 == t // 8) & (s <= t), (1, 4))
    masks = [base]
    for L in (8, 16):
        j = np.arange(64)[None, :]
        masks.append(np.tile((s // (2 * L) == j // L) & (s % (2 * L) < L), (1, 4)))
    return c, np.concatenate(masks, 1).astype(np.float32)


def columns(w):
    n = w.shape[1] // 128
    return w.reshape(8, 128, n, 128).transpose(2, 1, 0, 3).reshape(n, 128, 1024)


def groups(w):
    n = w.shape[1] // 512
    return w.reshape(4, 2, 128, n, 512).transpose(3, 0, 2, 1, 4).reshape(4 * n, 128, 1024)


def kernel(x, c, positions, w_ada, b_ada, g_pre_mix, g_post_mix, w_in, conv_w, w_out, g_pre_mlp,
           g_post_mlp, w_fc1, w_fc2, norm_g_2, pool_w_in_2, pool_w_grp_2, pool_scale_2, pool_w_out_2,
           hgrn_w_in_2, hgrn_lower_bounds_2, hgrn_norm_g_2, hgrn_w_out_2, final_g_2):
    import concourse.bacc as bacc
    from concourse.bass_utils import run_bass_kernel_spmd

    def col(v):
        return np.asarray(v).reshape(-1, 128).T

    cst, msk = constants()
    w1 = np.asarray(w_in)[0]
    q0 = 3 * 512
    order = [columns(w1[:, q0:q0 + 1024]), columns(w1[:, q0 + 1536:q0 + 2048])]
    parts = columns(w1[:, 0:1536])
    parts = parts[[3 * 0 + p * 4 + i - 0 for i in range(4) for p in (0, 2, 1)]]
    pin = np.asarray(pool_w_in_2)[0]
    grp = np.asarray(pool_w_grp_2)[0]
    pool = []
    for g in range(4):
        v = pin[:, 512 * g:512 * g + 512]
        pool.append(groups(v) if g == 0 else columns(v))
        pool.append(columns(pin[:, 2048 + 512 * g:2048 + 512 * g + 512]))
        pool.append(grp[g].reshape(4, 128, 2, 256).transpose(2, 1, 0, 3).reshape(2, 128, 1024))
    hin = np.asarray(hgrn_w_in_2)[0]
    qfg = np.stack([columns(hin[:, 2048:4096]), columns(hin[:, 0:2048]), columns(hin[:, 6144:8192])], 1)
    arrays = {
        "x": np.asarray(x)[0].T,
        "positions": np.asarray(positions),
        "vec": np.concatenate([
            col(c), col(b_ada), col(g_pre_mix), col(g_post_mix), col(g_pre_mlp), col(g_post_mlp),
            col(conv_w), col(norm_g_2), col(final_g_2), col(pool_scale_2), col(hgrn_lower_bounds_2),
            col(hgrn_norm_g_2)], 1),
        "cst": cst,
        "msk": msk,
        "ada": np.asarray(w_ada)[0].reshape(8, 128, 6, 1024).transpose(2, 0, 1, 3).reshape(48, 128, 1024),
        "w_in": np.concatenate([groups(w1[:, q0 + 1024:q0 + 1536]), *order, parts]),
        "w_out": np.asarray(w_out)[0].reshape(8, 128, 1024),
        "w_fc1": np.concatenate([groups(np.asarray(w_fc1)[0][:, 0:512]),
                                 columns(np.asarray(w_fc1)[0][:, 512:4096])]),
        "w_fc2": np.asarray(w_fc2)[0].reshape(32, 128, 1024),
        "pool_in": np.concatenate(pool),
        "pool_out": np.asarray(pool_w_out_2)[0].reshape(16, 128, 1024),
        "hgrn_in": np.concatenate([groups(hin[:, 4096:6144]), qfg.reshape(48, 128, 1024)]),
        "hgrn_out": np.concatenate([columns(np.asarray(hgrn_w_out_2)[0][0:1024]),
                                    np.asarray(hgrn_w_out_2)[0][1024:].reshape(8, 128, 1024)]),
    }
    arrays = {k: np.ascontiguousarray(v) for k, v in arrays.items()}
    nc = bacc.Bacc("TRN2", target_bir_lowering=False, num_devices=1)
    aps = {k: nc.dram_tensor(f"in_{k}", v.shape, mybir.dt.from_np(v.dtype), kind="ExternalInput").ap()
           for k, v in arrays.items()}
    aps["out"] = nc.dram_tensor("out", (1024, T), F32, kind="ExternalOutput").ap()
    build(nc, aps)
    r = run_bass_kernel_spmd(nc, [{f"in_{k}": v for k, v in arrays.items()}], core_ids=[0])
    return np.ascontiguousarray(r.results[0]["out"].T)[None]
```

```python
from contextlib import ExitStack

import concourse.bass as bass
import numpy as np
from concourse import mybir

F32 = mybir.dt.float32
F32R = mybir.dt.float32r
I32 = mybir.dt.int32
U8 = mybir.dt.uint8
ALU = mybir.AluOpType
ACT = mybir.ActivationFunctionType

T = 512
EPS = 1e-6
NR = 5
NS = 4
NZ = 3

V_C, V_BADA, V_GPRE1, V_GPOST1, V_GPRE2, V_GPOST2 = 0, 8, 56, 64, 72, 80
V_CONV, V_NG0, V_NG1, V_FG, V_PS, V_LB, V_HG, V_N = 88, 100, 108, 116, 124, 140, 172, 188
C_ID, C_FREQ, C_SGN, C_HPI, C_CNT, C_D = 0, 128, 129, 130, 131, 195
C_N = 195 + 4 * T


def unit_list():
    out = [("ada", 8 * j + k, False) for j in (1, 0) for k in range(8)]
    ada = iter(range(16, 48))
    for n in range(28):
        out.append(("w_in", n, True))
        if 1 <= n <= 24:
            out.append(("ada", next(ada), False))
    for name, n in (("w_out", 8), ("w_fc1", 32), ("w_fc2", 32), ("pool_in", 40), ("pool_out", 16),
                    ("hgrn_in", 64), ("hgrn_out", 16)):
        for i in range(n):
            out.append((name, i, True))
            if name == "w_fc1" and 6 <= i < 14:
                out.append(("ada", next(ada), False))
    return out


class Queue:

    def __init__(self, sem):
        self.sem, self.count, self.items, self.seen = sem, 0, [], {}

    def put(self, fn, *waits):
        todo = []
        for m in waits:
            if m is None:
                continue
            sem, value = m
            if self.seen.get(id(sem), 0) < value:
                self.seen[id(sem)] = value
                todo.append((sem, value))
        self.count += 1
        self.items.append((todo, fn))
        return self.sem, self.count

    def emit(self, eng):
        for todo, fn in self.items:
            for sem, value in todo:
                eng.wait_ge(sem, value)
            fn(eng).then_inc(self.sem, 1)


def build(nc, a):
    with ExitStack() as ctx:
        def sb(name, shape, dt=F32):
            return ctx.enter_context(nc.sbuf_tensor(name, shape, dt))

        def sem(name):
            return ctx.enter_context(nc.semaphore(name))

        X = sb("X", [128, 8, T])
        HH = sb("HH", [128, 8, T], F32R)
        HL = sb("HL", [128, 8, T], F32R)
        RAW = sb("RAW", [128, NR, 1024])
        WH = sb("WH", [128, NS, 1024], F32R)
        WL = sb("WL", [128, NS, 1024], F32R)
        Z = sb("Z", [128, 32, T])
        ZH = sb("ZH", [128, NZ, T], F32R)
        ZL = sb("ZL", [128, NZ, T], F32R)
        VEC = sb("VEC", [128, V_N])
        CST = sb("CST", [128, C_D])
        MSK = sb("MSK", [128, 1024], U8)
        ONES = sb("ONES", [128, 128])
        MOD = sb("MOD", [128, 48])
        COL = sb("COL", [128, 96])
        RB = sb("RB", [128, T])
        DG = sb("DG", [128, T])
        TMP = sb("TMP", [128, 5, T])
        NW = sb("NW", [128, 6, 16])
        NWI = sb("NWI", [128, 2, 16], I32)
        PS = [ctx.enter_context(nc.psum_tensor(f"PS{i}", [128, T], F32)) for i in range(8)]

        s_raw = [sem(f"s_raw{i}") for i in range(NR)]
        s_vec, s_cst, s_x, s_pos, s_d, s_msk, s_out = (
            sem(n) for n in ("s_vec", "s_cst", "s_x", "s_pos", "s_d", "s_msk", "s_out"))
        PE, DV, AC = (Queue(sem(n)) for n in ("s_pe", "s_dve", "s_act"))
        sp = []

        units = unit_list()
        split_of = [i for i, u in enumerate(units) if u[2]]
        freed = {}
        st = {"next": 0, "split": 0, "hi": 0, "unit": 0, "z": 0, "ada": 0}
        w_ready, w_used = {}, {}

        def load_unit(i):
            name, n, _ = units[i]
            m = freed.get(i - NR)
            sp.append(([m] if m else [], RAW[:, i % NR, :], a[name][n], s_raw[i % NR]))

        def landed(i):
            return s_raw[i % NR], 16 * (i // NR + 1)

        ACCS = [Z[:, 26 + 2 * i:28 + 2 * i, :].rearrange("p a b -> p (a b)") for i in range(2)]
        ada = {"acc": [None, None], "sum": None, "read": [None, None], "open": None}

        def sum_ada(i, n):
            j, k = divmod(n, 8)
            st["ada"] += 1
            src = RAW[:, i % NR, :]
            sc = COL[:, k:k + 1]
            b = j if j < 2 else 0
            ACC = ACCS[b]
            if k == 0:
                m = DV.put(lambda e: e.tensor_scalar(ACC, src, sc, None, ALU.mult),
                           landed(i), silu_c, ada["read"][b])
            else:
                m = DV.put(lambda e: e.scalar_tensor_tensor(out=ACC, in0=src, scalar=sc, in1=ACC,
                                                            op0=ALU.mult, op1=ALU.add),
                           landed(i), ada["acc"][b])
            ada["acc"][b] = m
            if k == 2:
                close_ada()
            if k == 7:
                def mm(e):
                    for c in range(8):
                        r = e.matmul(PS[7][:, 16 + c:17 + c], ACC[:, 128 * c:128 * c + 128], ONES[:, 0:1],
                                     start=True, stop=True)
                    return r
                ada["read"][b] = PE.put(mm, m, ones, ada["sum"], small["free"], bank_free[7])
                ada["open"] = j, b
            return m

        def close_ada():
            if ada["open"]:
                j, b = ada["open"]
                ada["open"] = None
                mod[j] = small["free"] = ada["sum"] = bank_free[7] = DV.put(
                    lambda e: e.tensor_tensor(MOD[:, 8 * j:8 * j + 8], PS[7][:, 16:24],
                                              VEC[:, V_BADA + 8 * j:V_BADA + 8 * j + 8], ALU.add),
                    ada["read"][b])

        def first_half():
            i = st["next"]
            if i >= len(units):
                return
            st["next"] += 1
            if units[i][2]:
                s = st["hi"]
                st["hi"] += 1
                hi = AC.put(lambda e: e.activation(WH[:, s % NS, :], RAW[:, i % NR, :], ACT.Copy),
                            landed(i), w_used.get(s - NS))
                halves.append((s, i, hi))
            else:
                freed[i] = sum_ada(i, units[i][1])
                if i + NR < len(units):
                    load_unit(i + NR)

        def second_half():
            s, i, hi = halves.pop(0)
            st["split"] += 1
            freed[i] = w_ready[s] = DV.put(
                lambda e: e.tensor_tensor(WL[:, s % NS, :], RAW[:, i % NR, :],
                                          WH[:, s % NS, :].bitcast(F32), ALU.subtract), hi)
            if i + NR < len(units):
                load_unit(i + NR)

        halves = []

        def prefetch(n):
            while st["hi"] < min(st["unit"] + n + 1, len(split_of)):
                first_half()
            while st["split"] < min(st["unit"] + n, len(split_of)):
                second_half()

        def unit():
            s = st["unit"]
            st["unit"] += 1
            prefetch(1)
            return s, s % NS

        mod, small = {}, {"free": None}
        bank_free = [None] * 8

        def three(e, out, wh, wl, xh, xl, first, last):
            e.matmul(out, wh, xh, start=first, stop=False)
            e.matmul(out, wh, xl, start=False, stop=False)
            return e.matmul(out, wl, xh, start=False, stop=last)

        def gemm4(banks, tokens, h_ready, evac):
            for q in range(4):
                s, slot = unit()
                wh = WH[:, slot, :].rearrange("p (k c) -> p k c", k=2)
                wl = WL[:, slot, :].rearrange("p (k c) -> p k c", k=2)
                for kk in range(2):
                    k = 2 * q + kk
                    for j in range(4):
                        cols = slice(128 * j, 128 * j + 128)

                        def mm(e, j=j, k=k, kk=kk, cols=cols, wh=wh, wl=wl):
                            if tokens:
                                return three(e, PS[banks[j]][:, :], HH[:, k, cols], HL[:, k, cols],
                                             wh[:, kk, :], wl[:, kk, :], k == 0, k == 7)
                            return three(e, PS[banks[j]][:, :], wh[:, kk, cols], wl[:, kk, cols],
                                         HH[:, k, :], HL[:, k, :], k == 0, k == 7)
                        m = PE.put(mm, w_ready[s], h_ready[k], bank_free[banks[j]] if k == 0 else None)
                        if k == 7:
                            evac(j, m)
                    if kk == 0:
                        prefetch(2)
                    yield
                w_used[s] = m

        def gemm1(bank, h_ready, evac, last=True):
            s, slot = unit()
            for k in range(8):
                cols = slice(128 * k, 128 * k + 128)
                m = PE.put(lambda e, k=k, cols=cols: three(
                    e, PS[bank][:, :], WH[:, slot, cols], WL[:, slot, cols], HH[:, k, :], HL[:, k, :],
                    k == 0, k == 7 and last), w_ready[s], h_ready[k], bank_free[bank] if k == 0 else None)
                if k == 3:
                    prefetch(2)
                if k == 7:
                    w_used[s] = m
                    evac(m)
                yield

        def run(main, *side):
            for n, _ in enumerate(main):
                for g in side:
                    next(g, None)

        def split_hi(src, n, ready):
            return AC.put(lambda e: e.activation(ZH[:, n % NZ, :], src, ACT.Copy), ready, z_used.get(n - NZ))

        def split_lo(src, n, hi):
            return DV.put(lambda e: e.tensor_tensor(ZL[:, n % NZ, :], src, ZH[:, n % NZ, :].bitcast(F32),
                                                    ALU.subtract), hi)

        z_used = {}

        def split_first(z_ready, k0=0):
            base = st["z"] - k0
            for k in range(k0, k0 + 2):
                split_early[k] = split_lo(Z[:, k, :], base + k,
                                          split_hi(Z[:, k, :], base + k, z_ready[k]))

        split_early = {}

        def gemm_out(nk, z_ready, evac, order=range(8), k0=0):
            if not split_early:
                split_first(z_ready, k0)
            ready = dict(split_early)
            split_early.clear()
            base = st["z"] - k0
            st["z"] += nk - k0
            for k in range(k0, nk):
                s, slot = unit()
                if k + 2 < nk:
                    hi = split_hi(Z[:, k + 2, :], base + k + 2, z_ready[k + 2])
                z = (base + k) % NZ
                for n, f in enumerate(order if k == nk - 1 else range(8)):
                    if n == 4 and k + 2 < nk:
                        ready[k + 2] = split_lo(Z[:, k + 2, :], base + k + 2, hi)
                    if n == (0 if k == nk - 1 else 6):
                        prefetch(2)
                    cols = slice(128 * f, 128 * f + 128)
                    m = PE.put(lambda e, f=f, k=k, cols=cols, z=z, slot=slot: three(
                        e, PS[f][:, :], WH[:, slot, cols], WL[:, slot, cols], ZH[:, z, :], ZL[:, z, :],
                        k == 0, k == nk - 1), w_ready[s], ready[k], bank_free[f] if k == 0 else None)
                    if k == nk - 1:
                        evac(f, m)
                w_used[s] = z_used[base + k] = m

        def column_sums(src, col, ready, first=True, last=True):
            close_ada()
            def mm(e):
                for j in range(4):
                    r = e.matmul(PS[7][:, col + j:col + j + 1], src[:, 128 * j:128 * j + 128], ONES[:, 0:1],
                                 start=first and j == 0, stop=last, skip_group_check=True)
                return r
            return PE.put(mm, ones, ready, small["free"] if first else None, bank_free[7] if first else None)

        def rsqrt(n, scale, ready):
            x, y, t, xh = (NW[:, i, 0:n] for i in (4, 1, 2, 3))
            i0, i1 = NWI[:, 0, 0:n], NWI[:, 1, 0:n]
            m = DV.put(lambda e: e.tensor_scalar(x, PS[7][:, 0:n], scale, EPS, ALU.mult, ALU.add),
                       ready, nw["used"])
            small["free"] = m
            m2 = DV.put(lambda e: e.tensor_single_scalar(i0, x.bitcast(I32), 1, ALU.logical_shift_right), m)
            m1 = DV.put(lambda e: e.tensor_scalar(xh, x, -0.5, None, ALU.mult), m)
            m = m2
            m = DV.put(lambda e: e.tensor_scalar(i1, i0, -1.0, 1597463007.0, ALU.mult, ALU.add), m)
            cur = i1.bitcast(F32)
            for it in range(3):
                src = cur
                m = DV.put(lambda e, src=src: e.tensor_tensor(t, src, src, ALU.mult), m)
                m = DV.put(lambda e: e.tensor_tensor(t, t, xh, ALU.mult), m, m1)
                dst = y if it % 2 else NW[:, 0, 0:n]
                m = DV.put(lambda e, src=src, dst=dst: e.scalar_tensor_tensor(
                    out=dst, in0=t, scalar=1.5, in1=src, op0=ALU.add, op1=ALU.mult), m)
                cur = dst
            return m

        nw = {"used": None}

        def diagonal(c0, ready):
            for j in range(4):
                m = DV.put(lambda e, j=j: e.tensor_scalar(
                    DG[:, 128 * j:128 * j + 128], IDN, NW[:, 0, c0 + j:c0 + j + 1], None, ALU.mult),
                    ready, dg["used"])
            nw["used"] = m
            return m

        def spread(bank, ready):
            dg["used"] = PE.put(lambda e: e.matmul(PS[bank][:, :], ONES[:, :], DG[:, :], start=True,
                                                   stop=True), ready, ones, bank_free[bank])
            return dg["used"]

        dg = {"used": None}
        rb = {"used": None}

        def factors(ready, copy=True):
            m = spread(6, diagonal(0, rsqrt(4, 1.0 / 1024, ready)))
            if not copy:
                return m
            m = AC.put(lambda e: e.activation(RB[:, :], PS[6][:, :], ACT.Copy), m, rb["used"])
            bank_free[6] = m
            return m

        tmp_free = [None] * 5
        h_used = {"m": None}

        def make_h(gain, shift, x_ready, *ready):
            out, his = [], {}
            prefetch(0)
            for k in range(9):
                if k < 8:
                    t = TMP[:, k % 2, :]
                    m = DV.put(lambda e, k=k, t=t: e.scalar_tensor_tensor(
                        out=t, in0=X[:, k, :], scalar=gain[:, k:k + 1], in1=PS[6][:, :], op0=ALU.mult,
                        op1=ALU.mult), *ready, x_ready[k], tmp_free[k % 2])
                    bank_free[6] = m
                    his[k] = AC.put(lambda e, k=k, t=t: e.activation(
                        HH[:, k, :], t, ACT.Identity, bias=shift[:, k:k + 1]), m, h_used["m"])
                if k in (1, 4):
                    prefetch(1 + k // 4)
                if k > 0:
                    j = k - 1
                    t = TMP[:, j % 2, :]
                    m = DV.put(lambda e, j=j, t=t: e.scalar_tensor_tensor(
                        out=HL[:, j, :], in0=t, scalar=shift[:, j:j + 1], in1=HH[:, j, :].bitcast(F32),
                        op0=ALU.add, op1=ALU.subtract), his[j])
                    tmp_free[j % 2] = m
                    out.append(m)
            return out

        def scaled(k, gain, ready):
            hi = AC.put(lambda e: e.activation(HH[:, k, :], X[:, k, :], ACT.Copy, scale=gain[:, k:k + 1]),
                        ready, h_used["m"])
            return lambda: DV.put(lambda e: e.scalar_tensor_tensor(
                out=HL[:, k, :], in0=X[:, k, :], scalar=gain[:, k:k + 1], in1=HH[:, k, :].bitcast(F32),
                op0=ALU.mult, op1=ALU.subtract), hi)

        def late_factors(x_ready, box):
            for k in range(8):
                m = square_acc(X[:, k, :], x_ready[k], k)
                if k < 6:
                    yield
            m = rsqrt(4, 1.0 / 1024, m)
            box["c"] = DV.put(lambda e: e.tensor_copy(COL[:, 88:92], NW[:, 0, 0:4]), m, rb["used"])
            d = diagonal(0, m)
            yield
            m = spread(6, d)
            box["r"] = bank_free[6] = AC.put(lambda e: e.activation(RB[:, :], PS[6][:, :], ACT.Copy),
                                             m, rb["used"])
            yield

        IDN = CST[:, C_ID:C_ID + 128]

        sp.append(([], VEC[:, :], a["vec"], s_vec))
        sp.append(([], CST[:, :], a["cst"][:, 0:C_D], s_cst))
        POSI = Z[:, 31, :].bitcast(I32)
        vec, cst, x_in = (s_vec, 16), (s_cst, 16), (s_x, 16)
        sp.append(([], X[:, :, :], a["x"].rearrange("(k p) t -> p k t", p=128), s_x))
        for i in range(NR):
            load_unit(i)
        sp.append(([], POSI, a["positions"].partition_broadcast(128), s_pos))
        DMASK = Z[:, 22:26, :]

        def late_loads():
            sp.append(([], Z[:, 0:2, :].rearrange("p a b -> p (a b)"), a["msk"], s_msk))
            sp.append(([], DMASK, a["cst"][:, C_D:C_N].rearrange("p (h t) -> p h t", h=4), s_d))

        ones = DV.put(lambda e: e.memset(ONES[:, :], 1.0))
        m = AC.put(lambda e: e.activation(COL[:, 8:16], VEC[:, V_C:V_C + 8], ACT.Sigmoid), vec)
        silu_c = DV.put(lambda e: e.tensor_tensor(COL[:, 0:8], COL[:, 8:16], VEC[:, V_C:V_C + 8],
                                                  ALU.mult), m, ones)

        def square(src, ready, k, ends=(7,), on=None):
            i = sum(e < k for e in ends)
            acc = SQ[:, i % 2, :]
            first = k == 0 or k - 1 in ends
            dst = acc if first else TMP[:, 2 + k % 2, :]
            free = sq_free[i % 2] if first else tmp_free[2 + k % 2]
            if on is None:
                m = AC.put(lambda e: e.activation(dst, src, ACT.Square), ready, free)
            else:
                m = on.put(lambda e: e.tensor_tensor(dst, src, src, ALU.mult), ready, free)

            def over_tiles(m=m):
                if not first:
                    m = DV.put(lambda e: e.tensor_tensor(acc, acc, dst, ALU.add), m, sq["acc"])
                    tmp_free[2 + k % 2] = m
                sq["acc"] = m

                def over_features():
                    if k in ends:
                        sq_free[i % 2] = column_sums(acc, 0, m, first=k == ends[0], last=k == 7)
                        return sq_free[i % 2]
                    return m
                return over_features
            return over_tiles

        def square_acc(*args):
            return square(*args)()()

        sq, sq_free = {"acc": None}, [None, None]
        SQ = sb("SQ", [128, 2, T])

        GA = COL[:, 16:24]
        for n in range(16):
            first_half()
            if n < 4:
                for k in (2 * n, 2 * n + 1):
                    m = square_acc(X[:, k, :], x_in, k, range(8))
            if n == 10:
                r1 = factors(m, copy=False)
                gain_ready = DV.put(lambda e: e.scalar_tensor_tensor(
                    out=GA, in0=MOD[:, 8:16], scalar=1.0, in1=VEC[:, V_GPRE1:V_GPRE1 + 8], op0=ALU.add,
                    op1=ALU.mult), mod[1])
        late_loads()

        COS, SIN = Z[:, 20, :], Z[:, 21, :]

        def angles():
            prefetch(0)
            ANG, TN = Z[:, 30, :], TMP[:, 4, :]
            m = DV.put(lambda e: e.tensor_copy(TN, POSI), (s_pos, 16))
            m = DV.put(lambda e: e.tensor_scalar(ANG, TN, CST[:, C_FREQ:C_FREQ + 1], None, ALU.mult), m, cst)
            m = DV.put(lambda e: e.tensor_scalar(TN, ANG, float(np.float32(1 / (2 * np.pi))), 12582912.0,
                                                 ALU.mult, ALU.add), m)
            m = DV.put(lambda e: e.tensor_scalar(TN, TN, 12582912.0, None, ALU.subtract), m)
            for i, part in enumerate(TWO_PI):
                if i >= 2:
                    yield
                m = DV.put(lambda e, part=part: e.scalar_tensor_tensor(
                    out=ANG, in0=TN, scalar=-part, in1=ANG, op0=ALU.mult, op1=ALU.add), m)
            yield
            msin = AC.put(lambda e: e.activation(SIN, ANG, ACT.Sin, scale=0.5), m)
            m = DV.put(lambda e: e.scalar_tensor_tensor(
                out=TN, in0=ANG, scalar=-1.0, in1=ANG, op0=ALU.mult, op1=ALU.max), m)
            yield
            m = AC.put(lambda e: e.activation(COS, TN, ACT.Sin, scale=-0.5, bias=CST[:, C_HPI:C_HPI + 1]), m)
            yield
            m1 = DV.put(lambda e: e.tensor_tensor(TN, SIN, SIN, ALU.mult), msin, m)
            yield
            m = DV.put(lambda e: e.scalar_tensor_tensor(out=SIN, in0=SIN, scalar=CST[:, C_SGN:C_SGN + 1],
                                                        in1=COS, op0=ALU.mult, op1=ALU.mult), m1)
            yield
            rot.append(DV.put(lambda e: e.tensor_scalar(COS, TN, -2.0, 1.0, ALU.mult, ALU.add), m))

        rot = []
        turns = angles()
        next(turns)
        prefetch(1)
        close_ada()

        h_ready = make_h(GA, MOD[:, 0:8], [x_in] * 8, r1, gain_ready, mod[0])

        z_ready = [None] * 32
        v_ready = [None] * 4
        VT = Z[:, 16:20, :]

        def evac_v(j, m):
            v_ready[j] = AC.put(lambda e: e.activation(VT[:, j, :], PS[j][:, :], ACT.Copy), m)
            bank_free[j] = v_ready[j]
        v_group = gemm4([0, 1, 2, 3], True, h_ready, evac_v)
        for _ in v_group:
            next(turns, None)
        for _ in turns:
            pass
        rot = rot[0]
        masks = DV.put(lambda e: e.tensor_copy(MSK[:, :], Z[:, 0:2, :].rearrange("p a b -> p (a b)")),
                       (s_msk, 16))

        qk_ready = [None] * 8

        def evac_rot(n, bank):
            def go(m):
                ps, b, out = PS[bank], TMP[:, n % 2, :], Z[:, 8 + n, :]
                DV.put(lambda e: e.tensor_tensor(b[0:64, :], ps[64:128, :], SIN[0:64, :], ALU.mult),
                       m, rot, tmp_free[n % 2])
                m1 = DV.put(lambda e: e.tensor_tensor(b[64:128, :], ps[0:64, :], SIN[64:128, :], ALU.mult), m)
                m2 = DV.put(lambda e: e.tensor_tensor(out, ps[:, :], COS, ALU.mult), m)
                bank_free[bank] = m2
                m = DV.put(lambda e: e.tensor_tensor(out, out, b, ALU.add), m1, m2)
                tmp_free[n % 2] = qk_ready[n] = m
            return go

        def evac_silu(dst, bank, done, owner=None):
            def go(m):
                m = AC.put(lambda e: e.activation(dst, PS[bank][:, :], ACT.Sigmoid), m,
                           owner and owner.free)
                m = DV.put(lambda e: e.tensor_tensor(dst, dst, PS[bank][:, :], ALU.mult), m)
                bank_free[bank] = m
                done(m)
            return go

        ring = [4, 5, 6]
        nb = 0
        for n in range(8):
            run(gemm1(ring[nb % 3], h_ready, evac_rot(n, ring[nb % 3])))
            nb += 1
        sg_ready = [None] * 4
        for n in range(4):
            def done(m, n=n):
                sg_ready[n] = m
            run(gemm1(ring[nb % 3], h_ready, evac_silu(Z[:, 4 + n, :], ring[nb % 3], done)))
            nb += 1

        def retention(h):
            A = Z[:, 28:31, :].rearrange("p a b -> p (a b)")
            off = [0, 512, 896, 1152]
            ready = []
            for i in range(4):
                n = T - 128 * i
                bank = i % 2
                m = PE.put(lambda e, i=i, n=n, bank=bank: e.matmul(
                    PS[bank][:, 0:n], Z[:, 12 + h, 128 * i:128 * i + 128], Z[:, 8 + h, 128 * i:T],
                    start=True, stop=True), qk_ready[h], qk_ready[4 + h], bank_free[bank])
                m = DV.put(lambda e, i=i, n=n, bank=bank: e.tensor_tensor(
                    A[:, off[i]:off[i] + n], PS[bank][:, 0:n], DMASK[:, h, 0:n], ALU.mult),
                    m, (s_d, 16), ret["a"], rot)
                bank_free[bank] = m
                ready.append(m)
                yield
                yield
            ob = 2 + h % 2
            for i in range(4):
                n = T - 128 * i
                m = PE.put(lambda e, i=i, n=n: e.matmul(
                    PS[ob][:, 128 * i:T], VT[:, i, 128 * h:128 * h + 128], A[:, off[i]:off[i] + n],
                    start=i == 0, stop=i == 3), ready[i], v_ready[i], bank_free[ob])
                yield
            yield
            ret["a"] = m
            t = TMP[:, 2 + h % 2, :]
            m1 = AC.put(lambda e: e.activation(t, PS[ob][:, :], ACT.Square), m, tmp_free[2 + h % 2])
            m2 = DV.put(lambda e: e.tensor_tensor(Z[:, 4 + h, :], PS[ob][:, :], Z[:, 4 + h, :], ALU.mult),
                        m, sg_ready[h], m1)
            bank_free[ob] = m2
            yield
            yield
            ret["sum"] = column_sums(t, 4 * h, m1, first=True)
            tmp_free[2 + h % 2] = ret["sum"]
            ret["z"][h] = m2
            yield
            yield

        ret = {"a": None, "sum": None, "z": [None] * 4}

        def ret_norm():
            m = rsqrt(16, 1.0 / 128, ret["sum"])
            for _ in range(8):
                yield
            for h in range(4):
                bank = h % 2
                d = diagonal(4 * h, m)
                yield
                yield
                yield
                m1 = spread(bank, d)
                z_ready[4 + h] = DV.put(lambda e, h=h, bank=bank: e.tensor_tensor(
                    Z[:, 4 + h, :], Z[:, 4 + h, :], PS[bank][:, :], ALU.mult), m1, ret["z"][h])
                bank_free[bank] = z_ready[4 + h]
                yield
                yield

        def chain(*gens):
            for g in gens:
                yield from g

        side = chain(*(retention(h) for h in range(4)), ret_norm())

        conv = {}

        def evac_x(i, bank):
            def go(m):
                conv["x"] = AC.put(lambda e: e.activation(TMP[:, 0, :], PS[bank][:, :], ACT.Copy),
                                   m, tmp_free[0])
                bank_free[bank] = conv["x"]
            return go

        def evac_c(i, bank):
            def go(m):
                u = TMP[:, 1, :]
                y = Z[:, i, :]
                w = [VEC[:, V_CONV + 4 * j + i:V_CONV + 4 * j + i + 1] for j in range(3)]
                m = DV.put(lambda e: e.tensor_tensor(u, TMP[:, 0, :], PS[bank][:, :], ALU.mult),
                           m, conv["x"], tmp_free[1])
                bank_free[bank] = tmp_free[0] = m
                m = DV.put(lambda e: e.tensor_scalar(y, u, w[2], None, ALU.mult), m)
                for j in (1, 2):
                    m = DV.put(lambda e, j=j: e.scalar_tensor_tensor(
                        out=y[:, j:T], in0=u[:, 0:T - j], scalar=w[2 - j], in1=y[:, j:T],
                        op0=ALU.mult, op1=ALU.add), m)
                tmp_free[1] = conv["y"] = m
            return go

        def evac_b(i, bank):
            def go(m):
                z_ready[i] = DV.put(lambda e: e.tensor_tensor(Z[:, i, :], Z[:, i, :], PS[bank][:, :],
                                                              ALU.mult), m, conv["y"])
                bank_free[bank] = z_ready[i]
            return go

        for i in range(4):
            for ev in (evac_x, evac_c, evac_b):
                if i == 3 and ev is evac_b:
                    split_first(z_ready)
                run(gemm1(ring[nb % 3], h_ready, ev(i, ring[nb % 3])), side)
                nb += 1
        for _ in side:
            pass
        h_used["m"] = (PE.sem, PE.count)
        while st["ada"] < 40:
            first_half()
        close_ada()

        def gains(dst, j, g, one):
            return DV.put(lambda e: e.scalar_tensor_tensor(
                out=COL[:, dst:dst + 8], in0=MOD[:, 8 * j:8 * j + 8], scalar=1.0 if one else 0.0,
                in1=VEC[:, g:g + 8], op0=ALU.add, op1=ALU.mult), mod[j])

        def residual(nk, z_ready, gate, gate_ready, x_ready, gain=None):
            y, sums = {}, []

            def evac(f, m):
                if f >= 6:
                    y[f] = (Z[:, f, :], AC.put(lambda e: e.activation(Z[:, f, :], PS[f][:, :], ACT.Copy), m))
                    bank_free[f] = y[f][1]
                else:
                    y[f] = (PS[f][:, :], m)
                sums.append(square_acc(y[f][0], y[f][1], len(sums), (7,), DV if f >= 6 else None))
            gemm_out(nk, z_ready, evac, [6, 7, 0, 1, 2, 3, 4, 5])
            r = factors(sums[-1])
            prefetch(2)
            out, h, low, squares = [], [], lambda: None, []
            for n, f in enumerate([6, 7, 0, 1, 2, 3, 4, 5] if gain is None else range(8)):
                t = TMP[:, n % 2, :]
                m = DV.put(lambda e, f=f, t=t: e.scalar_tensor_tensor(
                    out=t, in0=y[f][0], scalar=gate[:, f:f + 1], in1=RB[:, :], op0=ALU.mult,
                    op1=ALU.mult), r, y[f][1], gate_ready, tmp_free[n % 2])
                if f < 6:
                    bank_free[f] = m
                if squares:
                    squares.pop()()()
                m = DV.put(lambda e, f=f, t=t: e.tensor_tensor(X[:, f, :], X[:, f, :], t, ALU.add),
                           m, x_ready[f])
                tmp_free[n % 2] = m
                out.append((f, m))
                if gain is None:
                    squares.append(square(X[:, f, :], m, n, (1, 3, 5, 6, 7)))
                else:
                    h.append(low())
                    low = scaled(f, gain, m)
            rb["used"] = out[-1][1]
            if squares:
                m = squares.pop()()()
            x_ready = [m for _, m in sorted(out)]
            return x_ready, factors(m, copy=False) if gain is None else h[1:] + [low()]

        g1 = gains(32, 2, V_GPOST1, False)
        g2 = gains(40, 4, V_GPRE2, True)
        x_ready, r = residual(8, z_ready, COL[:, 32:40], g1, [x_in] * 8)

        h_ready = make_h(COL[:, 40:48], MOD[:, 24:32], x_ready, r, g2, mod[3])

        def evac_relu(f, bank):
            def go(m):
                t = TMP[:, f % 2, :]
                m = AC.put(lambda e: e.activation(t, PS[bank][:, :], ACT.Relu), m, tmp_free[f % 2])
                bank_free[bank] = m
                z_ready[f] = tmp_free[f % 2] = DV.put(
                    lambda e: e.tensor_tensor(Z[:, f, :], t, t, ALU.mult), m)
            return go
        run(gemm4([0, 1, 2, 3], False, h_ready, lambda j, m: evac_relu(j, j)(m)))
        for f in range(4, 32):
            if f == 18:
                close_ada()
            bank = f % 7
            if f == 31:
                split_first(z_ready)
            run(gemm1(bank, h_ready, evac_relu(f, bank)))
        h_used["m"] = (PE.sem, PE.count)
        g3 = gains(48, 5, V_GPOST2, False)
        x_ready, h_ready = residual(32, z_ready, COL[:, 48:56], g3, x_ready, VEC[:, V_NG0:V_NG0 + 8])

        r = h_ready[-1]
        norm = {}

        def with_factors(products, x_ready, evacs):
            late = late_factors(x_ready, norm)
            for _ in products:
                next(late, None)
            for _ in late:
                pass
            for go in evacs:
                go()
        PADW = 16 + T
        flat = Z[:, 20:32, :].rearrange("p a b -> p (a b)")
        VP, S1, S2, PP = (flat[:, PADW * i:PADW * (i + 1)] for i in range(4))
        pads = DV.put(lambda e: e.memset(
            flat[:, 0:4 * PADW].rearrange("p (i t) -> p i t", i=4)[:, :, 0:16], 0.0), r, (PE.sem, PE.count))
        pool = {"free": pads, "vp": pads, "p": {}, "g": {}}
        late = []

        def flush():
            while late:
                late.pop(0)()

        def window(g, j, bank):
            def go(m):
                w = 2 << g
                m = DV.put(lambda e: e.tensor_tensor(VP[:, 16:PADW], PS[bank][:, :], RB[:, :], ALU.mult),
                           m, pool["vp"], norm["r"])
                bank_free[bank] = m
                flush()
                src, dst = VP, S1
                for lev in range(g + 1):
                    sh = 1 << lev
                    m = DV.put(lambda e, src=src, dst=dst, sh=sh: e.tensor_tensor(
                        dst[:, 16:PADW], src[:, 16:PADW], src[:, 16 - sh:PADW - sh], ALU.add), m,
                        pool["free"])
                    src, dst = dst, (S2 if dst is S1 else S1)
                p = PP[:, 0:T]
                m1 = DV.put(lambda e: e.scalar_tensor_tensor(
                    out=p[:, 16:T], in0=src[:, 32:PADW], scalar=1.0 / w, in1=VP[:, 32:PADW],
                    op0=ALU.mult, op1=ALU.subtract), m)
                m2 = DV.put(lambda e: e.tensor_tensor(
                    p[:, 0:16], src[:, 16:32], CST[:, C_CNT + 16 * g:C_CNT + 16 * g + 16], ALU.mult), m)
                m = DV.put(lambda e: e.tensor_tensor(p[:, 0:16], p[:, 0:16], VP[:, 16:32], ALU.subtract), m2)
                pool["vp"] = m
                hi = AC.put(lambda e: e.activation(PHI(j), p, ACT.Copy), m, m1, grp["used"])

                def low():
                    pool["p"][j] = pool["free"] = DV.put(
                        lambda e: e.tensor_tensor(PLO(j), p, PHI(j).bitcast(F32), ALU.subtract), hi)
                late.append(low)
            return go

        def evac_silu_scaled(dst, bank, done, owner=None, later=None):
            def go(m):
                i = 3 + bank % 2 if later is late else 4
                t = TMP[:, i, :]
                m = DV.put(lambda e: e.tensor_tensor(t, PS[bank][:, :], RB[:, :], ALU.mult),
                           m, norm["r"], tmp_free[i])
                bank_free[bank] = m
                if later is late:
                    flush()
                m1 = AC.put(lambda e: e.activation(dst, t, ACT.Sigmoid), m, owner and owner.free)

                def last():
                    m = DV.put(lambda e: e.tensor_tensor(dst, dst, t, ALU.mult), m1)
                    tmp_free[i] = rb["used"] = m
                    done(m)
                if later is None:
                    last()
                else:
                    later.append(last)
            return go

        scope = ctx.enter_context(ExitStack())
        PSP = scope.enter_context(nc.sbuf_tensor("PSP", [128, 4, T], F32R))

        def PHI(j):
            return PSP[:, j, :]

        def PLO(j):
            return (ZH if j < 3 else ZL)[:, j % 3, :]
        grp = {"used": (PE.sem, PE.count)}
        for g in range(4):
            if g == 0:
                evacs = []
                first = gemm4([0, 1, 2, 3], False, h_ready,
                              lambda j, m: evacs.append(lambda: window(0, j, j)(m)))
            else:
                for j in range(4):
                    run(gemm1(j, h_ready, window(g, j, j)))
            for j in range(4):
                def done(m, j=j):
                    pool["g"][j] = m
                go = evac_silu_scaled(Z[:, 16 + j, :], 4 + j, done, None, late)
                if g == 0 and j == 0:
                    with_factors(chain(first, gemm1(4, h_ready, lambda m, go=go: evacs.append(
                        lambda: go(m)))), x_ready, evacs)
                else:
                    run(gemm1(4 + j, h_ready, go))
            flush()
            for q in range(2):
                s, slot = unit()
                wh = WH[:, slot, :].rearrange("p (k c) -> p k c", k=4)
                wl = WL[:, slot, :].rearrange("p (k c) -> p k c", k=4)
                for i in range(2):
                    f = 2 * q + i
                    bank = f
                    cols = slice(128 * i, 128 * i + 128)
                    for k in range(4):
                        m = PE.put(lambda e, k=k, bank=bank, cols=cols, wh=wh, wl=wl: three(
                            e, PS[bank][:, :], wh[:, k, cols], wl[:, k, cols], PHI(k), PLO(k),
                            k == 0, k == 3), w_ready[s], pool["p"][k], bank_free[bank] if k == 0 else None)
                    zt = 4 * g + f
                    z_ready[zt] = DV.put(lambda e, zt=zt, f=f, bank=bank: e.scalar_tensor_tensor(
                        out=Z[:, zt, :], in0=PS[bank][:, :], scalar=VEC[:, V_PS + zt:V_PS + zt + 1],
                        in1=Z[:, 16 + f, :], op0=ALU.mult, op1=ALU.mult), m, pool["g"][f])
                    bank_free[bank] = z_ready[zt]
                w_used[s] = m
            grp["used"] = m
        h_used["m"] = (PE.sem, PE.count)

        def add_out(nk, x_ready, gain, k0=0):
            out, h, todo, low = {}, [], [], [lambda: None]

            def evac(f, m):
                m = DV.put(lambda e: e.tensor_tensor(X[:, f, :], X[:, f, :], PS[f][:, :], ALU.add),
                           m, x_ready[f])
                bank_free[f] = m
                out[f] = m
                if gain is None:
                    while len(todo) > 1:
                        todo.pop(0)()
                    todo.append(square(X[:, f, :], m, len(out) - 1, (1, 3, 5, 6, 7))())
                else:
                    h.append(low[-1]())
                    low.append(scaled(f, gain, m))
            gemm_out(nk, z_ready, evac, range(8) if gain is not None else [7, 6, 0, 1, 2, 3, 4, 5], k0)
            for go in todo:
                m = go()
            return out, factors(m, copy=False) if gain is None else h[1:] + [low[-1]()]

        for i in range(3):
            z_used[st["z"] - 1 - i] = grp["used"]
        x_ready, h_ready = add_out(16, x_ready, VEC[:, V_NG1:V_NG1 + 8])

        L0, L1 = VEC[:, V_LB:V_LB + 16], VEC[:, V_LB + 16:V_LB + 32]
        E0, E1, MX = NW[:, 4, :], NW[:, 5, :], NW[:, 3, :]
        LBC, OMC = COL[:, 0:16], COL[:, 16:32]
        last = (DV.sem, DV.count)
        m = DV.put(lambda e: e.tensor_tensor(MX, L0, L1, ALU.max), last)
        m1 = DV.put(lambda e: e.tensor_tensor(E0, L0, MX, ALU.subtract), m)
        m2 = DV.put(lambda e: e.tensor_tensor(E1, L1, MX, ALU.subtract), m)
        m1 = AC.put(lambda e: e.activation(E0, E0, ACT.Exp), m1, m2)
        m2 = AC.put(lambda e: e.activation(E1, E1, ACT.Exp), m2)
        m = DV.put(lambda e: e.tensor_tensor(MX, E0, E1, ALU.add), m1, m2)
        m = DV.put(lambda e: e.reciprocal(MX, MX), m)
        m1 = DV.put(lambda e: e.tensor_tensor(E0, E0, MX, ALU.mult), m)
        m2 = DV.put(lambda e: e.tensor_tensor(E1, E1, MX, ALU.mult), m)
        m = DV.put(lambda e: e.tensor_tensor(MX, E0, E1, ALU.add), m1, m2)
        m = DV.put(lambda e: e.tensor_tensor(LBC, MX, E0, ALU.subtract), m)
        m = DV.put(lambda e: e.tensor_scalar(OMC, LBC, -1.0, 1.0, ALU.mult, ALU.add), m)
        lb_ready = DV.put(lambda e: e.tensor_scalar(LBC, LBC, 2.0 ** -24, None, ALU.max), m)
        nw["used"] = lb_ready

        norm.clear()
        hv_ready = [None] * 16
        z_last = (PE.sem, PE.count)
        for g in range(4):
            banks = [0, 1, 2, 3] if g % 2 == 0 else [4, 5, 6, 7]

            def evac_hv(j, m, g=g, banks=banks):
                m = AC.put(lambda e: e.activation(
                    Z[:, 4 * g:4 * g + 4, 128 * j:128 * j + 128],
                    PS[banks[j]][:, :].rearrange("p (h v) -> p h v", h=4), ACT.Copy,
                    scale=COL[:, 88 + j:89 + j]), m, z_last, norm["c"])
                bank_free[banks[j]] = m
                for h in range(4):
                    hv_ready[4 * g + h] = m
            if g == 0:
                evacs = []
                with_factors(gemm4(banks, True, h_ready,
                                   lambda j, m: evacs.append(lambda: evac_hv(j, m))), x_ready, evacs)
            else:
                run(gemm4(banks, True, h_ready, evac_hv))

        hflat = Z[:, 16:32, :].rearrange("p a b -> p (a b)")

        class Head:
            def __init__(self, b):
                base = 4096 * b
                self.A = hflat[:, base:base + 2048]
                self.wide = hflat[:, base:base + 2560]
                self.tot = hflat[:, base + 512:base + 640]
                self.q, self.f, self.k, self.sg = (
                    hflat[:, base + 2048 + T * i:base + 2560 + T * i] for i in range(4))
                self.free = DV.put(lambda e: e.memset(self.A, 0.0), z_last)
        heads = [Head(0), Head(1)]
        scope.close()
        QP0, QP1, W, IW = (sb(n, [128, T]) for n in ("QP0", "QP1", "W", "IW"))
        QP = [QP0, QP1]
        w3 = DV.put(lambda e: e.memset(W[:, :], 1.0), z_last)
        LVB, OB, RBK = [3, 4], 5, 6
        hz = [None] * 16
        lv = {"n": 0}
        w_free = {"m": w3}

        def parts(x, L):
            v = x.rearrange("p (n a l) -> p n a l", a=2, l=L)
            return v[:, :, 0, :], v[:, :, 1, :]

        def project(h):
            b = heads[h % 2]
            qp = QP[h % 2][:, :]
            col = slice(h, h + 1)

            def ev_f(m):
                m = DV.put(lambda e: e.tensor_tensor(b.f, PS[0][:, :], RB[:, :], ALU.mult),
                           m, b.free, norm["r"])
                bank_free[0] = m
                m2 = AC.put(lambda e: e.activation(b.k, b.f, ACT.Sigmoid, scale=-1.0), m, b.free)
                m1 = AC.put(lambda e: e.activation(b.f, b.f, ACT.Sigmoid), m, m2)
                b.sigmoids = m1, m2
                prep.append(prepare(h))

            def ev_q(m):
                b.q_ready = DV.put(lambda e: e.tensor_tensor(b.q, PS[1][:, :], RB[:, :], ALU.mult),
                                   m, b.free, norm["r"])
                bank_free[1] = b.q_ready

            def done(m):
                b.sg_ready = m
            yield from gemm1(0, h_ready, ev_f)
            yield from gemm1(1, h_ready, ev_q)
            yield from gemm1(2, h_ready, evac_silu_scaled(b.sg, 2, done, b, gates))

        def prepare(h):
            b = heads[h % 2]
            qp = QP[h % 2][:, :]
            col = slice(h, h + 1)
            m1, m2 = b.sigmoids
            m = DV.put(lambda e: e.tensor_scalar(b.f, b.f, OMC[:, col], LBC[:, col], ALU.mult,
                                                 ALU.add), m1, lb_ready)
            b.k_ready = DV.put(lambda e: e.tensor_scalar(b.k, b.k, OMC[:, col], None, ALU.mult), m2)
            yield
            w8 = W[:, :].rearrange("p (n l) -> p n l", l=8)
            f8 = b.f.rearrange("p (n l) -> p n l", l=8)
            m = DV.put(lambda e: e.tensor_copy(w8[:, :, 2:5:2], f8[:, :, 3:5]), m, w_free["m"])
            yield
            m = DV.put(lambda e: e.tensor_tensor(w8[:, :, 1:6:4], w8[:, :, 2:5:2], f8[:, :, 2:6:3],
                                                 ALU.mult), m)
            m = DV.put(lambda e: e.tensor_tensor(w8[:, :, 0:7:6], w8[:, :, 1:6:4], f8[:, :, 1:7:5],
                                                 ALU.mult), m)
            yield
            m1 = DV.put(lambda e: e.tensor_tensor(w8[:, :, 7], w8[:, :, 6], f8[:, :, 7], ALU.mult), m)
            b.tl_ready = DV.put(lambda e: e.tensor_tensor(b.tot[:, 64:128], w8[:, :, 0], f8[:, :, 0],
                                                          ALU.mult), m, b.free)
            for i in range(4):
                yield
                c = slice(128 * i, 128 * i + 128)
                b.w_ready = DV.put(lambda e, c=c: e.reciprocal(IW[:, c], W[:, c]), m1, w_free["m"])
            yield
            (q0, q1), (p0, p1), (w0, w1), (i0, i1), (k0, k1), (f0, f1) = (
                parts(x, 4) for x in (b.q, qp, W[:, :], IW[:, :], b.k, b.f))
            DV.put(lambda e: e.tensor_tensor(f0, k0, w0, ALU.mult), b.w_ready, b.k_ready, b.tl_ready)
            yield
            kt = DV.put(lambda e: e.tensor_tensor(f1, k1, i1, ALU.mult), b.w_ready)
            yield
            DV.put(lambda e: e.tensor_tensor(p0, q0, i0, ALU.mult), b.w_ready, b.q_ready, b.free)
            b.t_ready = DV.put(lambda e: e.tensor_tensor(p1, q1, w1, ALU.mult), b.w_ready)
            w8 = W[:, :].rearrange("p (n l) -> p n l", l=8)
            v8 = [x.rearrange("p (n l) -> p n l", l=8) for x in (b.q, qp, b.k, b.f)]
            tl = b.tot[:, 64:128].rearrange("p (n o) -> p n o", o=1)
            yield
            m1 = DV.put(lambda e: e.tensor_tensor(
                v8[0], v8[1], tl.broadcast_to([128, 64, 8]), ALU.mult), b.t_ready)
            yield
            m2 = DV.put(lambda e: e.tensor_tensor(
                v8[2], v8[3], w8[:, :, 7:8].broadcast_to([128, 64, 8]), ALU.mult), kt)
            m3 = DV.put(lambda e: e.tensor_tensor(b.tot[:, 0:64], w8[:, :, 7], b.tot[:, 64:128],
                                                  ALU.mult), b.tl_ready, m1)
            w_free["m"] = m3
            b.q8_ready, b.k8_ready, b.tot_ready = m1, m2, m3

        def mixing(h):
            b = heads[h % 2]
            qp = QP[h % 2]
            diag = b.wide.rearrange("p (i t) -> p i t", i=4)

            def bank_of_level():
                lv["n"] += 1
                return LVB[lv["n"] % 2]
            bank = bank_of_level()
            ps = PS[bank]

            def mm(e, ps=ps):
                for i in range(4):
                    c = slice(128 * i, 128 * i + 128)
                    r = e.matmul(ps[:, c], b.f[:, c], qp[:, c], start=True, stop=True)
                return r
            m = PE.put(mm, b.t_ready, bank_free[bank])
            a_ready = DV.put(lambda e, ps=ps: e.copy_predicated(
                diag[:, :, 0:128], MSK[:, 0:512].rearrange("p (i t) -> p i t", i=4),
                ps[:, :].rearrange("p (i t) -> p i t", i=4)), m, masks)
            bank_free[bank] = a_ready
            q_ready, k_ready, t_ready = b.q8_ready, b.k8_ready, b.tot_ready
            tot, at = b.tot[:, 0:64], 64
            yield
            for L in (8, 16, 32, 64, 128, 256):
                bank = bank_of_level()
                ps = PS[bank]
                k0, q1 = parts(b.k, L)[0], parts(b.q, L)[1]
                if L <= 32:
                    def mm(e, L=L, ps=ps):
                        for i in range(4):
                            c = slice(128 * i, 128 * i + 128)
                            o = ps[:, 64 * i:64 * i + 64].rearrange("p (n l) -> p n l", l=L)
                            r = e.matmul(o, b.k[:, c], parts(b.q[:, c], L)[1], start=True, stop=True)
                        return r
                elif L == 64:
                    def mm(e, ps=ps, k0=k0, q1=q1):
                        for i in range(4):
                            r = e.matmul(ps[0:64, 64 * i:64 * i + 64], k0[:, i, :], q1[:, i, :],
                                         start=True, stop=True)
                        return r
                elif L == 128:
                    def mm(e, ps=ps, k0=k0, q1=q1):
                        for i in range(2):
                            r = e.matmul(ps[:, 128 * i:128 * i + 128], k0[:, i, :], q1[:, i, :],
                                         start=True, stop=True)
                        return r
                else:
                    def mm(e, ps=ps):
                        for i in range(2):
                            r = e.matmul(ps[:, 256 * i:256 * i + 256], b.k[:, 128 * i:128 * i + 128],
                                         b.q[:, 256:512], start=True, stop=True)
                        return r
                used = PE.put(mm, q_ready, k_ready, bank_free[bank])
                if L < 256:
                    n = T // (2 * L)
                    tv = tot.rearrange("p (n a) -> p n a", a=2)
                    q_ready = DV.put(lambda e, q1=q1, tv=tv, n=n, L=L: e.tensor_tensor(
                        q1, q1, tv[:, :, 0:1].broadcast_to([128, n, L]), ALU.mult), used, t_ready, q_ready)
                    k_ready = DV.put(lambda e, k0=k0, tv=tv, n=n, L=L: e.tensor_tensor(
                        k0, k0, tv[:, :, 1:2].broadcast_to([128, n, L]), ALU.mult), used, t_ready, k_ready)
                    if L < 128:
                        nt = b.tot[:, at:at + n]
                        at += n
                        t_ready = DV.put(lambda e, nt=nt, tv=tv: e.tensor_tensor(
                            nt, tv[:, :, 0], tv[:, :, 1], ALU.mult), t_ready)
                        tot = nt
                if L <= 16:
                    ad = diag[:, :, 0:128].rearrange("p i (n a l) -> p i n a l", a=2, l=L)[:, :, :, 1, :]
                    o = 512 + 256 * (L // 16)
                    a_ready = DV.put(lambda e, ad=ad, ps=ps, o=o, L=L: e.copy_predicated(
                        ad, MSK[:, o:o + 256].rearrange("p (i n l) -> p i n l", i=4, l=L),
                        ps[:, 0:256].rearrange("p (i n l) -> p i n l", i=4, l=L)), used, a_ready)
                    m = a_ready
                elif L == 32:
                    for i in range(2):
                        s0 = 64 * i
                        m = AC.put(lambda e, i=i, s0=s0, ps=ps: e.activation(
                            diag[s0:s0 + 32, :, s0 + 32:s0 + 64],
                            ps[s0:s0 + 32, 0:256].rearrange("p (i t) -> p i t", i=4)[:, :, 32 * i:32 * i + 32],
                            ACT.Copy), used, a_ready)
                elif L == 64:
                    m = AC.put(lambda e, ps=ps: e.activation(
                        diag[0:64, :, 64:128], ps[0:64, 0:256].rearrange("p (i t) -> p i t", i=4),
                        ACT.Copy), used, a_ready)
                elif L == 128:
                    m = AC.put(lambda e, ps=ps: e.activation(
                        b.A[:, 128:1536].rearrange("p (x t) -> p x t", t=128)[:, 0:11:10, :],
                        ps[:, 0:256].rearrange("p (x t) -> p x t", t=128), ACT.Copy), used)
                else:
                    m = AC.put(lambda e, ps=ps: e.activation(
                        b.A[:, 0:1024].rearrange("p (x t) -> p x t", x=2)[:, :, 256:512],
                        ps[:, :].rearrange("p (x t) -> p x t", x=2), ACT.Copy), used)
                bank_free[bank] = m
                yield

            def pv(e):
                o, v = PS[OB], Z[:, h, :]
                for i in range(4):
                    r = e.matmul(o[:, 128 * i:T], v[:, 128 * i:128 * i + 128],
                                 b.A[:, 640 * i:512 * i + 512], start=i == 0, stop=i == 3)
                return r
            m = PE.put(pv, m, hv_ready[h], bank_free[OB])
            t = TMP[:, 2 + h % 2, :]
            m1 = AC.put(lambda e: e.activation(t, PS[OB][:, :], ACT.Square), m, tmp_free[2 + h % 2])
            hz[h] = DV.put(lambda e: e.scalar_tensor_tensor(
                out=Z[:, h, :], in0=PS[OB][:, :], scalar=VEC[:, V_HG + h:V_HG + h + 1], in1=b.sg,
                op0=ALU.mult, op1=ALU.mult), m, b.sg_ready, m1)
            bank_free[OB] = b.free = hz[h]
            yield
            m = column_sums(t, 4 * (h % 4), m1)
            tmp_free[2 + h % 2] = m
            if h % 4 == 3:
                m = rsqrt(16, 1.0 / 128, m)
                norms.append(norm4(h - 3, m))
            yield

        def norm4(h, m):
            for i in range(4):
                d = diagonal(4 * i, m)
                yield
                m1 = spread(RBK, d)
                z_ready[h + i] = DV.put(lambda e, i=i: e.tensor_tensor(
                    Z[:, h + i, :], Z[:, h + i, :], PS[RBK][:, :], ALU.mult), m1, hz[h + i])
                bank_free[RBK] = z_ready[h + i]
                yield

        norms, prep, gates, parts_z = [], [], [], [None] * 8
        SIDE = (1, 3, 5, 8, 11, 14, 17, 19, 21, 23)

        def split_z(k):
            hi = AC.put(lambda e: e.activation(HH[:, k, :], Z[:, k, :], ACT.Copy), z_ready[k], h_free[k])
            parts_z[k] = DV.put(lambda e: e.tensor_tensor(
                HL[:, k, :], Z[:, k, :], HH[:, k, :].bitcast(F32), ALU.subtract), hi)

        def out_columns(bank):
            return gemm1(bank, parts_z, lambda m: None, False)
        h_free = {}
        turn, side, ready = iter(()), iter(()), iter(())
        for h in range(17):
            for n, _ in enumerate(project(h) if h < 16 else chain(*(out_columns(f) for f in range(3)))):
                if h == 15 and n >= 16:
                    h_free[n - 16] = (PE.sem, PE.count)
                    if n >= 20:
                        split_z(n - 20)
                if h == 16 and n < 3:
                    for k in ((4, 5), (6,), (7,))[n]:
                        split_z(k)
                if n == 10 and prep:
                    ready = prep.pop()
                if n >= 10 or h:
                    next(ready, None)
                if n == 3 and gates:
                    gates.pop()()
                if n in SIDE:
                    next(side, None)
                    next(turn, None)
                if n == 0 and h:
                    side = mixing(h - 1)
                    turn = norms.pop() if norms else turn
            for _ in ready:
                pass
            for _ in side:
                pass
        turn = norms.pop()
        for f in range(3, 6):
            for n, _ in enumerate(out_columns(f)):
                if n % 2:
                    next(turn, None)
        for _ in turn:
            pass
        run(out_columns(6))
        split_first(z_ready, 8)
        run(out_columns(7))
        x_ready, r = add_out(16, x_ready, None, 8)
        for f in range(8):
            m = DV.put(lambda e, f=f: e.scalar_tensor_tensor(
                out=Z[:, 16 + f, :], in0=X[:, f, :], scalar=VEC[:, V_FG + f:V_FG + f + 1], in1=PS[6][:, :],
                op0=ALU.mult, op1=ALU.mult), r, x_ready[f])
            sp.append(([m], a["out"][128 * f:128 * f + 128, :], Z[:, 16 + f, :], s_out))

        block = ctx.enter_context(nc.Block())

        @block.sync
        def _(e):
            for waits, dst, src, s in sp:
                for w in waits:
                    e.wait_ge(*w)
                e.dma_start(dst, src).then_inc(s, 16)
            e.wait_ge(s_out, 16 * 8)

        @block.tensor
        def _(e):
            PE.emit(e)

        @block.vector
        def _(e):
            DV.emit(e)

        @block.scalar
        def _(e):
            AC.emit(e)


def two_pi():
    rest, out = 2 * np.pi, []
    for _ in range(3):
        e = np.floor(np.log2(rest)) - 7
        part = np.floor(rest / 2.0 ** e) * 2.0 ** e
        out.append(float(part))
        rest -= part
    return out + [float(np.float32(rest))]


TWO_PI = two_pi()


def constants():
    c = np.zeros((128, C_N), np.float32)
    c[:, C_ID:C_ID + 128] = np.eye(128)
    half = np.arange(64, dtype=np.float32) / np.float32(64)
    c[:, C_FREQ] = np.tile((10000.0 ** -half.astype(np.float64)).astype(np.float32), 2)
    c[0:64, C_SGN], c[64:128, C_SGN] = -2.0, 2.0
    c[:, C_HPI] = np.pi / 2
    for g in range(4):
        c[:, C_CNT + 16 * g:C_CNT + 16 * g + 16] = 1.0 / np.minimum(np.arange(16) + 1.0, 2 << g)
    m, t = np.arange(128)[:, None], np.arange(T)[None, :]
    same = m // 64 == t // 64
    for h in range(4):
        gamma = 1.0 - 2.0 ** (-5.0 - h)
        d = np.where(same, gamma ** np.abs(t - m), np.where(t > m, gamma ** np.maximum(t - m, 0), 0.0))
        c[:, C_D + T * h:C_D + T * h + T] = d * 128.0 ** -0.5
    s, t = np.arange(128)[:, None], np.arange(128)[None, :]
    base = np.tile((s // 8 == t // 8) & (s <= t), (1, 4))
    masks = [base]
    for L in (8, 16):
        j = np.arange(64)[None, :]
        masks.append(np.tile((s // (2 * L) == j // L) & (s % (2 * L) < L), (1, 4)))
    return c, np.concatenate(masks, 1).astype(np.float32)


def columns(w):
    n = w.shape[1] // 128
    return w.reshape(8, 128, n, 128).transpose(2, 1, 0, 3).reshape(n, 128, 1024)


def groups(w):
    n = w.shape[1] // 512
    return w.reshape(4, 2, 128, n, 512).transpose(3, 0, 2, 1, 4).reshape(4 * n, 128, 1024)


def kernel(x, c, positions, w_ada, b_ada, g_pre_mix, g_post_mix, w_in, conv_w, w_out, g_pre_mlp,
           g_post_mlp, w_fc1, w_fc2, norm_g_2, pool_w_in_2, pool_w_grp_2, pool_scale_2, pool_w_out_2,
           hgrn_w_in_2, hgrn_lower_bounds_2, hgrn_norm_g_2, hgrn_w_out_2, final_g_2):
    import concourse.bacc as bacc
    from concourse.bass_utils import run_bass_kernel_spmd

    def col(v):
        return np.asarray(v).reshape(-1, 128).T

    cst, msk = constants()
    w1 = np.asarray(w_in)[0]
    q0 = 3 * 512
    order = [columns(w1[:, q0:q0 + 1024]), columns(w1[:, q0 + 1536:q0 + 2048])]
    parts = columns(w1[:, 0:1536])
    parts = parts[[4 * p + i for i in range(4) for p in (0, 2, 1)]]
    pin = np.asarray(pool_w_in_2)[0]
    grp = np.asarray(pool_w_grp_2)[0]
    pool = []
    for g in range(4):
        v = pin[:, 512 * g:512 * g + 512]
        pool.append(groups(v) if g == 0 else columns(v))
        pool.append(columns(pin[:, 2048 + 512 * g:2048 + 512 * g + 512]))
        pool.append(grp[g].reshape(4, 128, 2, 256).transpose(2, 1, 0, 3).reshape(2, 128, 1024))
    hin = np.asarray(hgrn_w_in_2)[0]
    qfg = np.stack([columns(hin[:, 2048:4096]), columns(hin[:, 0:2048]), columns(hin[:, 6144:8192])], 1)
    arrays = {
        "x": np.asarray(x)[0].T,
        "positions": np.asarray(positions),
        "vec": np.concatenate([
            col(c), col(b_ada), col(g_pre_mix), col(g_post_mix), col(g_pre_mlp), col(g_post_mlp),
            col(conv_w), col(norm_g_2), col(final_g_2), col(pool_scale_2), col(hgrn_lower_bounds_2),
            col(hgrn_norm_g_2)], 1),
        "cst": cst,
        "msk": msk,
        "ada": np.asarray(w_ada)[0].reshape(8, 128, 6, 1024).transpose(2, 0, 1, 3).reshape(48, 128, 1024),
        "w_in": np.concatenate([groups(w1[:, q0 + 1024:q0 + 1536]), *order, parts]),
        "w_out": np.asarray(w_out)[0].reshape(8, 128, 1024),
        "w_fc1": np.concatenate([groups(np.asarray(w_fc1)[0][:, 0:512]),
                                 columns(np.asarray(w_fc1)[0][:, 512:4096])]),
        "w_fc2": np.asarray(w_fc2)[0].reshape(32, 128, 1024),
        "pool_in": np.concatenate(pool),
        "pool_out": np.asarray(pool_w_out_2)[0].reshape(16, 128, 1024),
        "hgrn_in": np.concatenate([groups(hin[:, 4096:6144]), qfg.reshape(48, 128, 1024)]),
        "hgrn_out": np.concatenate([columns(np.asarray(hgrn_w_out_2)[0][0:1024]),
                                    np.asarray(hgrn_w_out_2)[0][1024:].reshape(8, 128, 1024)]),
    }
    arrays = {k: np.ascontiguousarray(v) for k, v in arrays.items()}
    nc = bacc.Bacc("TRN2", target_bir_lowering=False, num_devices=1)
    aps = {k: nc.dram_tensor(f"in_{k}", v.shape, mybir.dt.from_np(v.dtype), kind="ExternalInput").ap()
           for k, v in arrays.items()}
    aps["out"] = nc.dram_tensor("out", (1024, T), F32, kind="ExternalOutput").ap()
    build(nc, aps)
    r = run_bass_kernel_spmd(nc, [{f"in_{k}": v for k, v in arrays.items()}], core_ids=[0])
    return np.ascontiguousarray(r.results[0]["out"].T)[None]
```
